# Optimizing a Trainium2 kernel written in Bass

```python
import functools
import jax, jax.numpy as jnp
from jax import lax
import numpy as np

D_MODEL = 1024
BATCH = 1
SEQ = 1024
DEPTH = 1
DEC_BATCH = 8
DEC_SEQ = 1
PAST_LEN = 1024
PAGE_SIZE = 128

N_META = 16
N_HEADS = 8
HEAD_DIM = 64
ATTN_DIM = N_HEADS * HEAD_DIM
IDX_HEADS = 4
IDX_DIM = 64
IDX_SCALE = (IDX_HEADS * IDX_DIM) ** -0.5
TOPK_MAX = 256
CONV_DIM = 512
CONV_WIDTH = 3
D_FF = 2816
FFN_CONV_WIDTH = 3
ROPE_THETA = 10000.0
EPS = 1e-6
Q_BLOCK = 128
IN_SIZES = (ATTN_DIM, ATTN_DIM, ATTN_DIM, IDX_HEADS * IDX_DIM, IDX_DIM, IDX_HEADS,
            CONV_DIM, CONV_DIM, CONV_DIM, D_MODEL, D_MODEL)
IN_COLS = sum(IN_SIZES)

kernel_name = 'hybrid_dsa_shortconv_decode_step'

def rms_norm(x, w):
    xf = x.astype(jnp.float32)
    y = xf * lax.rsqrt(jnp.mean(xf * xf, axis=-1, keepdims=True) + EPS)
    return (y * w.astype(jnp.float32)).astype(x.dtype)

def rope(x, pos):
    d = x.shape[-1]
    half = d // 2
    freqs = ROPE_THETA ** (-jnp.arange(half, dtype=jnp.float32) / half)
    ang = pos.astype(jnp.float32)[:, None] * freqs[None, :]
    cos = jnp.cos(ang)[None, :, None, :]
    sin = jnp.sin(ang)[None, :, None, :]
    xf = x.astype(jnp.float32)
    x1, x2 = xf[..., :half], xf[..., half:]
    return jnp.concatenate([x1 * cos - x2 * sin, x1 * sin + x2 * cos], axis=-1).astype(x.dtype)

def causal_dwconv(u_hist, w):
    width = w.shape[0]
    n = u_hist.shape[1] - (width - 1)
    out = u_hist[:, 0:n] * w[0]
    for j in range(1, width):
        out = out + u_hist[:, j:j + n] * w[j]
    return out

def indexer_scores(qi, wi, ki):
    s = jnp.einsum('bqhd,bsd->bqhs', qi.astype(jnp.float32), ki.astype(jnp.float32))
    return jnp.einsum('bqhs,bqh->bqs', jax.nn.relu(s), wi.astype(jnp.float32)) * IDX_SCALE

def sparse_softmax(q, kg, vg, valid):
    logits = jnp.einsum('bqhd,bqkhd->bqhk', q.astype(jnp.float32), kg.astype(jnp.float32)) * (HEAD_DIM ** -0.5)
    logits = jnp.where(valid[:, :, None, :], logits, -jnp.inf)
    p = jax.nn.softmax(logits, axis=-1)
    return jnp.einsum('bqhk,bqkhd->bqhd', p, vg.astype(jnp.float32)).astype(q.dtype)

def prompt_sparse_attention(q, k, v, qi, wi, ki, topk):
    B, T = q.shape[0], q.shape[1]
    n_blk = -(-T // Q_BLOCK)
    t_pad = n_blk * Q_BLOCK

    def to_blocks(a):
        a = jnp.pad(a, [(0, 0), (0, t_pad - T)] + [(0, 0)] * (a.ndim - 2))
        return jnp.moveaxis(a.reshape((B, n_blk, Q_BLOCK) + a.shape[2:]), 1, 0)

    key_pos = jnp.arange(T, dtype=jnp.int32)

    def body(args):
        qb, qib, wib, start = args
        qpos = start + jnp.arange(Q_BLOCK, dtype=jnp.int32)
        sc = indexer_scores(qib, wib, ki)
        causal = key_pos[None, :] <= qpos[:, None]
        sc = jnp.where(causal[None], sc, -jnp.inf)
        _, sel = lax.top_k(sc, topk)
        valid = sel <= qpos[None, :, None]
        kg = jax.vmap(lambda kb, ib: kb[ib])(k, sel)
        vg = jax.vmap(lambda vb, ib: vb[ib])(v, sel)
        return sparse_softmax(qb, kg, vg, valid)

    starts = jnp.arange(n_blk, dtype=jnp.int32) * Q_BLOCK
    out = lax.map(body, (to_blocks(q), to_blocks(qi), to_blocks(wi), starts))
    return jnp.moveaxis(out, 0, 1).reshape(B, t_pad, N_HEADS, HEAD_DIM)[:, :T]

def sample_sparse_attention(q, k_new, v_new, qi, wi, ki_new, cache_k, cache_v, cache_kidx, page_table, topk):
    DB, S = q.shape[0], q.shape[1]
    past = page_table.shape[1] * PAGE_SIZE
    L = past + S
    ki_past = cache_kidx[page_table].reshape(DB, past, IDX_DIM)
    ki_all = jnp.concatenate([ki_past.astype(ki_new.dtype), ki_new], axis=1)
    qpos = past + jnp.arange(S, dtype=jnp.int32)
    sc = indexer_scores(qi, wi, ki_all)
    causal = jnp.arange(L, dtype=jnp.int32)[None, :] <= qpos[:, None]
    sc = jnp.where(causal[None], sc, -jnp.inf)
    _, sel = lax.top_k(sc, topk)
    valid = sel <= qpos[None, :, None]
    in_past = (sel < past)[..., None, None]
    ps = jnp.minimum(sel, past - 1)
    phys = jax.vmap(lambda pt, i: pt[i])(page_table, ps // PAGE_SIZE)
    off = ps % PAGE_SIZE
    ns = jnp.clip(sel - past, 0, S - 1)
    kg = jnp.where(in_past, cache_k[phys, off].astype(k_new.dtype), jax.vmap(lambda kb, ib: kb[ib])(k_new, ns))
    vg = jnp.where(in_past, cache_v[phys, off].astype(v_new.dtype), jax.vmap(lambda vb, ib: vb[ib])(v_new, ns))
    return sparse_softmax(q, kg, vg, valid)

def trunk_layer(x, pos, conv_prev, ffn_prev, attend, attn_norm_w, w_in, q_norm_w, k_norm_w, conv_w,
                w_o_attn, w_o_conv, w_merge, ffn_norm_w, w_up, ffn_conv_w, ffn_conv_b, w_down):
    B, T = x.shape[0], x.shape[1]
    xn = rms_norm(x, attn_norm_w)
    split_at = np.cumsum(IN_SIZES)[:-1].tolist()
    q, k, v, qi, ki, wi, cx, cb, cc, ga, gc = jnp.split(xn @ w_in, split_at, axis=-1)
    q = rope(rms_norm(q.reshape(B, T, N_HEADS, HEAD_DIM), q_norm_w), pos)
    k = rope(rms_norm(k.reshape(B, T, N_HEADS, HEAD_DIM), k_norm_w), pos)
    v = v.reshape(B, T, N_HEADS, HEAD_DIM)
    qi = rope(qi.reshape(B, T, IDX_HEADS, IDX_DIM), pos)
    ki = rope(ki[:, :, None, :], pos)[:, :, 0]
    attn = attend(q, k, v, qi, wi, ki).reshape(B, T, ATTN_DIM)
    u_hist = jnp.concatenate([conv_prev.astype(x.dtype), cc * cx], axis=1)
    conv_out = cb * causal_dwconv(u_hist, conv_w)
    conv_state = u_hist[:, -(CONV_WIDTH - 1):]
    mixed = jax.nn.sigmoid(ga) * (attn @ w_o_attn) + jax.nn.sigmoid(gc) * (conv_out @ w_o_conv)
    h = x + mixed @ w_merge
    hn = rms_norm(h, ffn_norm_w)
    g, val = jnp.split(hn @ w_up, [D_FF], axis=-1)
    g_hist = jnp.concatenate([ffn_prev.astype(x.dtype), g], axis=1)
    g_conv = causal_dwconv(g_hist, ffn_conv_w) + ffn_conv_b
    y = h + (jax.nn.silu(g_conv) * val) @ w_down
    ffn_state = g_hist[:, -(FFN_CONV_WIDTH - 1):]
    return y, k, v, ki, conv_state, ffn_state

def setup_inputs(seed: int = 0) -> dict:
    key = jax.random.key(seed)
    ks = jax.random.split(key, 24)
    n_pages = PAST_LEN // PAGE_SIZE
    n_phys = (DEC_BATCH * n_pages * 5) // 4
    nrm = lambda k, shape, scale=1.0: jax.random.normal(k, shape, jnp.float32) * scale
    page_table = jax.random.permutation(ks[7], n_phys)[:DEC_BATCH * n_pages].reshape(DEC_BATCH, n_pages).astype(jnp.int32)
    return {
        'x_prompt': nrm(ks[0], (BATCH, SEQ, D_MODEL)),
        'x_sample': nrm(ks[1], (DEC_BATCH, DEC_SEQ, D_MODEL)),
        'cache_k': nrm(ks[2], (DEPTH, n_phys, PAGE_SIZE, N_HEADS, HEAD_DIM)),
        'cache_v': nrm(ks[3], (DEPTH, n_phys, PAGE_SIZE, N_HEADS, HEAD_DIM)),
        'cache_kidx': nrm(ks[4], (DEPTH, n_phys, PAGE_SIZE, IDX_DIM)),
        'state_conv': nrm(ks[5], (DEPTH, DEC_BATCH, CONV_WIDTH - 1, CONV_DIM)),
        'state_ffn_conv': nrm(ks[6], (DEPTH, DEC_BATCH, FFN_CONV_WIDTH - 1, D_FF)),
        'page_table': page_table,
        'meta_tokens': nrm(ks[8], (N_META, D_MODEL)),
        'attn_norm_w': 1.0 + nrm(ks[9], (DEPTH, D_MODEL), 0.01),
        'w_in': nrm(ks[10], (DEPTH, D_MODEL, IN_COLS), D_MODEL ** -0.5),
        'q_norm_w': 1.0 + nrm(ks[11], (DEPTH, HEAD_DIM), 0.01),
        'k_norm_w': 1.0 + nrm(ks[12], (DEPTH, HEAD_DIM), 0.01),
        'conv_w': nrm(ks[13], (DEPTH, CONV_WIDTH, CONV_DIM), CONV_WIDTH ** -0.5),
        'w_o_attn': nrm(ks[14], (DEPTH, ATTN_DIM, D_MODEL), ATTN_DIM ** -0.5),
        'w_o_conv': nrm(ks[15], (DEPTH, CONV_DIM, D_MODEL), CONV_DIM ** -0.5),
        'w_merge': nrm(ks[16], (DEPTH, D_MODEL, D_MODEL), D_MODEL ** -0.5),
        'ffn_norm_w': 1.0 + nrm(ks[17], (DEPTH, D_MODEL), 0.01),
        'w_up': nrm(ks[18], (DEPTH, D_MODEL, 2 * D_FF), D_MODEL ** -0.5),
        'ffn_conv_w': nrm(ks[19], (DEPTH, FFN_CONV_WIDTH, D_FF), FFN_CONV_WIDTH ** -0.5),
        'ffn_conv_b': nrm(ks[20], (DEPTH, D_FF), 0.01),
        'w_down': nrm(ks[21], (DEPTH, D_FF, D_MODEL), D_FF ** -0.5),
    }

def reference(x_prompt, x_sample, cache_k, cache_v, cache_kidx, state_conv, state_ffn_conv, page_table,
              meta_tokens, attn_norm_w, w_in, q_norm_w, k_norm_w, conv_w, w_o_attn, w_o_conv, w_merge,
              ffn_norm_w, w_up, ffn_conv_w, ffn_conv_b, w_down):
    B = x_prompt.shape[0]
    DB, S = x_sample.shape[0], x_sample.shape[1]
    past = page_table.shape[1] * PAGE_SIZE
    topk_p = min(TOPK_MAX, x_prompt.shape[1] // 4)
    topk_s = min(TOPK_MAX, (past + S) // 4)
    hp = jnp.concatenate([jnp.broadcast_to(meta_tokens.astype(x_prompt.dtype)[None], (B, N_META, D_MODEL)), x_prompt], axis=1)
    T = hp.shape[1]
    pos_p = jnp.arange(T, dtype=jnp.int32)
    pos_s = past + jnp.arange(S, dtype=jnp.int32)
    hs = x_sample
    kp, vp, kip, cp, fp = [], [], [], [], []
    ksm, vsm, kism, csm, fsm = [], [], [], [], []
    for l in range(DEPTH):
        wl = (attn_norm_w[l], w_in[l], q_norm_w[l], k_norm_w[l], conv_w[l], w_o_attn[l], w_o_conv[l],
              w_merge[l], ffn_norm_w[l], w_up[l], ffn_conv_w[l], ffn_conv_b[l], w_down[l])
        attend_p = functools.partial(prompt_sparse_attention, topk=topk_p)
        hp, k1, v1, ki1, c1, f1 = trunk_layer(
            hp, pos_p, jnp.zeros((B, CONV_WIDTH - 1, CONV_DIM), hp.dtype),
            jnp.zeros((B, FFN_CONV_WIDTH - 1, D_FF), hp.dtype), attend_p, *wl)
        attend_s = functools.partial(sample_sparse_attention, cache_k=cache_k[l], cache_v=cache_v[l],
                                     cache_kidx=cache_kidx[l], page_table=page_table, topk=topk_s)
        hs, k2, v2, ki2, c2, f2 = trunk_layer(hs, pos_s, state_conv[l], state_ffn_conv[l], attend_s, *wl)
        kp.append(k1); vp.append(v1); kip.append(ki1); cp.append(c1); fp.append(f1)
        ksm.append(k2); vsm.append(v2); kism.append(ki2); csm.append(c2); fsm.append(f2)
    y_prompt = hp[:, N_META:]
    y_sample = hs
    return (y_prompt, y_sample,
            jnp.stack(kp), jnp.stack(vp), jnp.stack(kip), jnp.stack(cp), jnp.stack(fp),
            jnp.stack(ksm), jnp.stack(vsm), jnp.stack(kism), jnp.stack(csm), jnp.stack(fsm))


_drawn_inputs = setup_inputs


def setup_inputs(seed=0):
    import zlib

    import numpy as np

    out = dict(_drawn_inputs(seed))
    spreads = {}
    factors = {'attn_norm_w': 4.272,
     'q_norm_w': 64.0,
     'k_norm_w': 38.898,
     'ffn_norm_w': 33.674,
     'ffn_conv_b': 45.814,
     'cache_k': 3.222,
     'cache_v': 3.324,
     'cache_kidx': 3.5}
    for name, (base, spread) in spreads.items():
        noise = np.random.default_rng([zlib.crc32(name.encode()), seed]).standard_normal(out[name].shape)
        drawn = base * np.exp(spread * noise) if base else spread * noise
        out[name] = __import__('jax').numpy.asarray(drawn.astype(out[name].dtype))
    for name, factor in factors.items():
        out[name] = (out[name] * factor).astype(out[name].dtype)
    return out
```

```python
from contextlib import ExitStack

import numpy as np

import concourse.bass as bass
from concourse import mybir

F32 = mybir.dt.float32
F32R = mybir.dt.float32r
I32 = mybir.dt.int32
ALU = mybir.AluOpType
ACT = mybir.ActivationFunctionType
AX = mybir.AxisListType
ds = bass.ds

P = 128
D = 1024
KD = D // P
NMETA = 16
TPR = 1040
NS = 8
T = TPR + NS
CH = 352
NCH = 3
TP = CH * NCH
NH, HD = 8, 64
IH = 4
NB = 9
LR = 24
PAGES = 8
PAST = PAGES * P
DFF = 2816
NF = DFF // P
TOPK = 256
EPS = 1e-6
NEG = -1.0e30
TAKEN = -3.0e38

N_KI, N_QI, N_KQ, N_V, N_CONV, N_GATE, N_O, N_MERGE, N_UP = 0, 1, 3, 11, 15, 27, 43, 51, 59
N_TILES = N_UP + 2 * NF

C_ID, C_ONES, C_CM, C_E24, C_OH, C_BD, C_NM, C_DIAG, C_ZP, C_ROWP, C_EPS, C_CM8 = (
    0, 128, 256, 384, 448, 456, 968, 992, 1000, 1032, 1033, 1034)
C_SEL = C_CM8 + 32
C_END = C_SEL + 128
W_AN, W_FN, W_QK, W_CW, W_CS, W_FW, W_FB, W_FS = 0, 8, 16, 24, 36, 100, 166, 188
W_END = W_FS + NF * 16

S_W = [P * (b + 1) for b in range(8)] + [TP]
S_OFF = {}
_o = 0
for _b in range(2, NB):
    S_OFF[_b] = _o
    _o += S_W[_b]
S_TOTAL = _o
ROWS = [P] * 8 + [LR]


def _t_copy(copy, dst, px, k0, nk, width, rows, done):
    if width - k0 * P >= nk * P:
        src = px[:, 0:nk * P].rearrange("p (t q) -> p t q", t=nk)[:, :, 0:rows]
        copy(dst[:, k0:k0 + nk, 0:rows], src).then_inc(done, 1)
    else:
        w = width - k0 * P
        copy(dst[0:w, k0, 0:rows], px[0:w, 0:rows]).then_inc(done, 1)


def build(nc, io):
    ctx = ExitStack()
    with ctx:
        base = -(-nc.sbuf_base // 32) * 32
        arena = ctx.enter_context(nc.sbuf_tensor("arena", [P, (nc.sbuf_usable_end - base) // 4 - 16], F32))

        def at(name, shape, off, dt=F32):
            n = 4
            for s in shape[1:]:
                n *= s
            assert base + off + n <= nc.sbuf_usable_end, (name, off, n)
            return nc.alloc_sbuf_tensor_at(name, shape, dt, offset=base + off)

        R = 4 * TP
        WRAW = [at(f"WRAW{b}", [P, KD, P], 4096 * b) for b in range(2)]
        WHI = [at(f"WHI{b}", [P, KD, P], 8192 + 4096 * b, F32R) for b in range(2)]
        WLO = [at(f"WLO{b}", [P, KD, P], 16384 + 4096 * b, F32R) for b in range(2)]
        o1 = 24576
        XT = at("XT", [P, KD, TP], o1)
        QKT = at("QKT", [P, 8, TP], o1)
        o2 = o1 + 8 * R
        VT = at("VT", [P, NB, 512], o2)
        o3 = o2 + NB * 2048
        ROT = [at(f"ROT{b}", [P, TP], o3 + b * R) for b in range(2)]
        COS = at("COS", [P, TP], o3 + 2 * R)
        SIN = at("SIN", [P, TP], o3 + 3 * R)
        ACC = at("ACC", [P, TP], o3 + 4 * R)
        S = at("S", [P, S_TOTAL], o3)
        SELT = at("SELT", [16, 8, P], o3 + 5 * R)
        o4 = o3 + 6 * R
        EV = [at(f"EV{b}", [P, TP], o4 + b * R) for b in range(2)]
        QS = [at(f"QS{h}", [P, NB * P], o1 + 4608 * h, F32R) for h in range(IH)]
        KH2 = at("KH2", [P, TP], o1 + 18432, F32R)
        KL2 = at("KL2", [P, TP], o1 + 18432 + R, F32R)
        KIP = [at(f"KIP{b}", [P, 4, P], o1 + 26880 + 2048 * b) for b in range(2)]
        QZ = at("QZ", [P, NS, 32], o1 + 30976)
        ZZ = at("ZZ", [LR, 32], o1 + 32000)
        WDS = at("WDS", [32, LR], o1 + 32128)
        RD = at("RD", [32, 1024], o1 + 18432)
        o5 = o4 + 2 * R
        KIDX = at("KIDX", [P, NS * PAGES, HD], o5)
        KIO = at("KIO", [HD, TP], o5 + 16384)
        COS2 = at("COS2", [P, TP], o2)
        SIN2 = at("SIN2", [P, TP], o2 + R)
        ROT2 = [at(f"ROT2{b}", [P, TP], o2 + (2 + b) * R) for b in range(2)]
        SQ = at("SQ", [P, TP], o5)
        RS = at("RS", [16, TP], o5 + R)
        CB = at("CB", [P, TP], o5)
        U = at("U", [P, TP + 2], o5 + R)
        TC = [at(f"TC{j}", [P, TP], o5 + 2 * R + 64 + j * R) for j in range(3)]
        o7 = 134080
        XH = at("XH", [P, KD, TP], o7, F32R)
        XL = at("XL", [P, KD, TP], o7 + 8 * R, F32R)
        oc = o7 + 16 * R
        CK = at("CK", [P, C_END], oc)
        WV = at("WV", [P, W_END], oc + 4800)
        om = oc + 4800 + 2176
        WI = at("WI", [P, NB, IH], om)
        UT = at("UT", [P, 4, 10], om + 160)
        GT = at("GT", [P, NF, 10], om + 320)
        PT = at("PT", [1, NS * PAGES], om + 1216, I32)
        SM = at("SM", [P, 64], om + 1472)
        M8 = [at(f"M8{j}", [P, 8], om + 1728 + 32 * j) for j in range(2)]
        SELC = [at(f"SELC{j}", [P, 16], om + 1792 + 64 * j) for j in range(2)]
        RT = at("RT", [P, NB], om + 1920)
        QPAD = [QS[h][:, TP:NB * P].bitcast(F32) for h in range(IH)]
        PB = [at(f"PB{b}", [P, TP], 97920 + b * R) for b in range(2)]
        PTB = [at(f"PTB{b}", [P, NB, P], 106368 + 4608 * b) for b in range(2)]
        oh = (115584, 0)
        HQ = [at(f"HQ{b}", [P, NB * P], oh[b], F32R) for b in range(2)]
        HKH = [at(f"HKH{b}", [P, TP], oh[b] + 4608, F32R) for b in range(2)]
        HKL = [at(f"HKL{b}", [P, TP], oh[b] + 4608 + R, F32R) for b in range(2)]
        LD = at("LD", [P, PAGES, NS, NH], 128640)
        QTOK = at("QTOK", [32, 512], 130688)
        VLAST = at("VLAST", [32, P], 132736)
        QA = at("QA", [P, 4, 64], 16384)
        RING = [at(f"RING{b}", [P, PAGES, 512], 134080 + 16384 * b) for b in range(2)]
        QB = at("QB", [P, NS, 512], 166848)
        AT = at("AT", [P, NB, 512], 183232)
        PZ = at("PZ", [P, PAGES * NS * 64 + 64], 97920)
        PD = at("PD", [64, TP], 114560)
        MREP = at("MREP", [64, TP], 118784)
        OD = at("OD", [64, 512], 123008)
        PTN = at("PTN", [LR, 64], 125056)
        AH = at("AH", [P, 4, TP], o1, F32R)
        AL = at("AL", [P, 4, TP], o1 + 4 * R, F32R)
        COH = at("COH", [P, 4, TP], o2, F32R)
        COL = at("COL", [P, 4, TP], o2 + 4 * R, F32R)
        og = o2 + 8 * R
        SGA = [at(f"SGA{b}", [P, TP], og + b * R) for b in range(2)]
        SGC = [at(f"SGC{b}", [P, TP], og + (2 + b) * R) for b in range(2)]
        MT = [at(f"MT{b}", [P, TP], og + (4 + b) * R) for b in range(2)]
        CRAW = [at(f"CRAW{b}", [P, TP], og + (6 + b) * R) for b in range(2)]
        XR = [at(f"XR{b}", [P, TP], o2 + b * R) for b in range(2)]
        HSQ = [at(f"HSQ{b}", [P, TP], o2 + (2 + b) * R) for b in range(2)]
        HACC = at("HACC", [P, TP], o2 + 4 * R)
        HT_ = [at(f"HT{b}", [P, TP], o2 + (5 + b) * R) for b in range(2)]
        FH = at("FH", [P, 2, TP], o2, F32R)
        FL = at("FL", [P, 2, TP], o2 + 2 * R, F32R)
        of = o2 + 4 * R
        DRAW = at("DRAW", [P, 2, D], of)
        DHI = at("DHI", [P, 2, D], of + 8192, F32R)
        DLO = at("DLO", [P, 2, D], of + 16384, F32R)
        G = [at(f"G{b}", [P, TP + 2], of + 24576 + 4256 * b) for b in range(2)]
        TG = [at(f"TG{b}", [P, TP], of + 33088 + R * b) for b in range(2)]
        assert of + 33088 + 2 * R <= 134080

        PS = [ctx.enter_context(nc.psum_tensor(f"PS{b}", [P, NCH, 512], F32)) for b in range(2)]
        PX = [ctx.enter_context(nc.psum_tensor(f"PX{b}", [P, 512], F32)) for b in range(2)]
        ps_all = [t[:, :, 0:CH] for t in PS]

        def v3(ap):
            return ap.rearrange("p (c t) -> p c t", c=NCH)

        ident = CK[:, C_ID:C_ID + P]
        ones = CK[:, C_ONES:C_ONES + P]
        eps = CK[:, C_EPS:C_EPS + 1]

        xt_d, ws_d, wd_d = io["xT"], io["wtiles"], io["wdown"]
        gates_d = nc.dram_tensor("gates", (16, P, TP), F32, kind="Internal").ap()
        q_d = nc.dram_tensor("decode_q", (1, NS * 512), F32, kind="Internal").ap()
        conv_d = nc.dram_tensor("convout", (4, P, TP), F32, kind="Internal").ap()

        def sem(name):
            return ctx.enter_context(nc.semaphore(name))

        w_raw = [sem(f"w_raw{b}") for b in range(2)]
        w_hi = [sem(f"w_hi{b}") for b in range(2)]
        w_lo = [sem(f"w_lo{b}") for b in range(2)]
        mm = [sem(f"mm{b}") for b in range(2)]
        ps_free = [sem(f"ps_free{b}") for b in range(2)]
        const_in, wv_in, rope_in, pt_in = sem("const_in"), sem("wv_in"), sem("rope_in"), sem("pt_in")
        x_in = [sem(f"x_in{k}") for k in range(KD)]
        n_sq, n_acc, n_sum, n_rt, n_rc, n_bc, n_t, n_hi, n_lo, n_lop = (
            sem(s) for s in ("n_sq", "n_acc", "n_sum", "n_rt", "n_rc", "n_bc", "n_t", "n_hi", "n_lo", "n_lop"))
        i_rot, i_cos, i_sin, i_out, i_hi, i_lo, qs_pad = (
            sem(s) for s in ("i_rot", "i_cos", "i_sin", "i_out", "i_hi", "i_lo", "qs_pad"))
        r_ev, r_rot, r_sin, r_cos, r_out, r_ms, r_rt, r_rc, r_bc, r_nrm = (
            sem(s) for s in ("r_ev", "r_rot", "r_sin", "r_cos", "r_out", "r_ms", "r_rt", "r_rc", "r_bc", "r_nrm"))
        act_step, dve_step, pool_step = sem("act_step"), sem("dve_step"), sem("pool_step")
        wi_t, wi_c = sem("wi_t"), sem("wi_c")
        rope2_in, r_ev2 = sem("rope2_in"), sem("r_ev2")
        sc_mm, sc_relu, sc_acc = sem("sc_mm"), sem("sc_relu"), sem("sc_acc")
        kidx_in, qz_c, kip_t, kip_c, di_mm, di_relu, zz_c, zz_t, wds_c, ds_mm, s8_c = (
            sem(s) for s in ("kidx_in", "qz_c", "kip_t", "kip_c", "di_mm", "di_relu", "zz_c", "zz_t", "wds_c", "ds_mm", "s8_c"))
        v_t, v_c = sem("v_t"), sem("v_c")
        c_u, c_t, c_out = sem("c_u"), sem("c_t"), sem("c_out")
        c_dma = sem("c_dma")
        g_dma = [sem(f"g_dma{b}") for b in range(2)]
        held = sem("held")
        out_done, k_saved, ki_saved, v_saved = (sem(s) for s in ("out_done", "k_saved", "ki_saved", "v_saved"))
        q_t, q_c, q_dma, qb_in, qa_c, pool_ready = (
            sem(s) for s in ("q_t", "q_c", "q_dma", "qb_in", "qa_c", "pool_ready"))
        ring_in = [sem(f"ring_in{b}") for b in range(2)]
        k_prod, k_red, v_pv = sem("k_prod"), sem("k_red"), sem("v_pv")
        masks_made, hd_hi, hd_lo, a_vl, a_qk, a_lg, a_max, a_nm, a_exp, a_rc, a_tm, a_ta, a_td, a_pv, a_o = (
            sem(s) for s in ("masks_made", "hd_hi", "hd_lo", "a_vl", "a_qk", "a_lg", "a_max", "a_nm", "a_exp", "a_rc", "a_tm", "a_ta", "a_td", "a_pv", "a_o"))
        d_mr, d_mrc, d_l, d_p, d_exp, d_t, d_c, d_o, d_at, at_t, at_h, at_l = (
            sem(s) for s in ("d_mr", "d_mrc", "d_l", "d_p", "d_exp", "d_t", "d_c", "d_o", "d_at", "at_t", "at_h", "at_l"))
        co_in = [sem(f"co_in{b}") for b in range(2)]
        co_h, co_l = sem("co_h"), sem("co_l")
        sg_in = [sem(f"sg_in{b}") for b in range(2)]
        o_ps, o_m0, o_m1, o_mix, o_hi, o_lo = (sem(s) for s in ("o_ps", "o_m0", "o_m1", "o_mix", "o_hi", "o_lo"))
        xr_in = [sem(f"xr_in{b}") for b in range(2)]
        h_out = sem("h_out")
        f_g, f_t0, f_s, f_cv, f_si, f_a, f_hi, f_lo = (sem(s) for s in ("f_g", "f_t0", "f_s", "f_cv", "f_si", "f_a", "f_hi", "f_lo"))
        d_raw, d_hi, d_lo, d_mm, d_px = sem("d_raw"), sem("d_hi"), sem("d_lo"), sem("d_mm"), sem("d_px")

        block = ctx.enter_context(nc.Block())

        UNITS = [(b, e) for e in range(2) for b in range(NB)]
        FREE = 2
        NU = len(UNITS)
        KT_N = [-(-S_W[b] // P) for b in range(NB)]
        BATCHES = []
        _n = 0
        for b, e in UNITS:
            mine = []
            for k0 in range(0, KT_N[b], 4):
                mine.append((_n, k0, min(4, KT_N[b] - k0)))
                _n += 1
            BATCHES.append(mine)
        NBAT = _n
        assert NBAT % 2 == 0 and NU % 2 == 0

        def unit(u, i):
            return (u, i) if u < NU else (u - NU, i + 1)

        @block.sync
        def _(sp):
            sp.dma_start(CK[:, :], io["consts"]).then_inc(const_in, 16)
            for k in range(KD):
                sp.dma_start(XT[:, k, :], xt_d[:, k, :]).then_inc(x_in[k], 16)
            sp.dma_start(WV[:, :], io["smallw"]).then_inc(wv_in, 16)

            def load(n, b):
                sp.dma_start(WRAW[b][:, :, :].rearrange("p k m -> p (k m)"),
                             ws_d[ds(n, 1), :, :].rearrange("a p m -> p (a m)")).then_inc(w_raw[b], 16)

            load(0, 0)
            load(1, 1)
            sp.dma_start(COS[:, :], io["cos"]).then_inc(rope_in, 16)
            sp.dma_start(SIN[:, :], io["sin"]).then_inc(rope_in, 16)
            sp.dma_start(PT[:, :], io["page_table"]).then_inc(pt_in, 16)
            sp.wait_ge(pt_in, 16)

            def indexer_pages(j0, j1):
                with sp.Fori(j0, j1) as j:
                    page = sp.value_load(PT[0:1, ds(j, 1)], min_val=0, max_val=79)
                    sp.dma_start(KIDX[:, ds(j, 1), :].rearrange("p a d -> p (a d)"),
                                 io["cache_kidx"][ds(page, 1), :, :].rearrange("a p d -> p (a d)")).then_inc(kidx_in, 16)

            indexer_pages(0, 20)
            sp.wait_ge(w_lo[0], 1)
            load(2, 0)
            indexer_pages(20, 40)
            sp.wait_ge(w_lo[1], 1)
            load(3, 1)
            sp.dma_start(COS2[:, :], io["cos"]).then_inc(rope2_in, 16)
            sp.dma_start(SIN2[:, :], io["sin"]).then_inc(rope2_in, 16)
            sp.dma_start(SELT[:, :, :], io["selt"]).then_inc(rope2_in, 16)
            indexer_pages(40, NS * PAGES)

            def weights(n0, n1):
                with sp.Fori(n0 // 2, n1 // 2) as k:
                    for b in range(2):
                        sp.wait_ge(w_lo[b], k)
                        load(2 * k + b, b)

            weights(4, N_O - 1)
            sp.wait_ge(w_lo[0], 21)
            load(N_O - 1, 0)
            sp.wait_ge(mm[0], 22)
            sp.wait_ge(q_dma, 16)
            sp.dma_start(QB[:, :, :].rearrange("p s d -> p (s d)"), q_d.to_broadcast([P, NS * 512])).then_inc(qb_in, 16)

            def pages(cache, s, b, v):
                for p in range(PAGES):
                    page = sp.value_load(PT[0:1, ds(s * PAGES + p, 1)], min_val=0, max_val=79)
                    sp.dma_start(RING[b][:, p, :],
                                 cache[ds(page, 1), :, :].rearrange("a p d -> p (a d)")).then_inc(ring_in[b], 16)

            pages(io["cache_k"], 0, 0, 0)
            pages(io["cache_k"], 1, 1, 0)
            with sp.Fori(1, NS // 2) as i:
                for b in range(2):
                    sp.wait_ge(k_red, i * 16 - 8 + 8 * b)
                    pages(io["cache_k"], 2 * i + b, b, 0)
            for b in range(2):
                sp.wait_ge(k_red, 56 + 8 * b)
                pages(io["cache_v"], b, b, 1)
            sp.wait_ge(a_qk, 4 * NU)
            load(N_O, 1)
            load(N_O + 1, 0)
            with sp.Fori(1, NS // 2) as i:
                for b in range(2):
                    sp.wait_ge(v_pv, 2 * i - 1 + b)
                    pages(io["cache_v"], 2 * i + b, b, 1)
            sp.wait_ge(c_dma, 64)
            sp.wait_ge(at_l, NB + 1)
            for j in range(4):
                if j >= 2:
                    sp.wait_ge(co_l, j - 1)
                sp.dma_start(CRAW[j % 2][:, :], conv_d[j, :, :]).then_inc(co_in[j % 2], 16)
            for b in range(2):
                sp.wait_ge(g_dma[b], 128)

            def load_next(n, b, k):
                sp.wait_ge(w_lo[b], k)
                load(n, b)

            def out_tiles(m, a, first):
                if not first:
                    sp.wait_ge(o_mix, m + a - 1)
                sp.dma_start(SGA[a][:, :], gates_d[ds(m + a, 1), :, :].rearrange("a p t -> p (a t)")).then_inc(sg_in[a], 16)
                sp.dma_start(SGC[a][:, :], gates_d[ds(m + a + 8, 1), :, :].rearrange("a p t -> p (a t)")).then_inc(sg_in[a], 16)

            for a in range(2):
                out_tiles(0, a, True)
                load_next(N_O + 2 + a, 1 - a, 22 + a)
            with sp.Fori(1, 4) as i:
                for a in range(2):
                    out_tiles(2 * i, a, False)
                    load_next(N_O + 2 + 2 * i + a, 1 - a, 22 + i + a)
            sp.wait_ge(mm[0], 26)
            for a in range(2):
                sp.dma_start(XR[a][:, :], xt_d[:, a, :]).then_inc(xr_in[a], 16)
                load_next(N_MERGE + 2 + a, 1 - a, 26 + a)
            with sp.Fori(1, 4) as i:
                for a in range(2):
                    sp.wait_ge(h_out, 2 * i + a - 1)
                    sp.dma_start(XR[a][:, :], xt_d[:, ds(2 * i + a, 1), :].rearrange("p a t -> p (a t)")).then_inc(xr_in[a], 16)
                    load_next(N_MERGE + 2 + 2 * i + a, 1 - a, 26 + i + a)
            sp.wait_ge(n_lo, 8)
            sp.wait_ge(n_lop, 8)

            def mixer(i, first, last):
                if not first:
                    sp.wait_ge(d_lo, i)
                sp.dma_start(DRAW[:, :, :], wd_d[ds(2 * i, 2), :, :].rearrange("a p m -> p a m")).then_inc(d_raw, 16)
                for q in range(2 if last else 4):
                    load_next(N_UP + 2 + 4 * i + q, 1 - q % 2, 30 + 2 * i + (q + 1) // 2)

            mixer(0, True, False)
            with sp.Fori(1, NF // 2 - 1) as i:
                mixer(i, False, False)
            mixer(NF // 2 - 1, False, True)
            sp.wait_ge(f_t0, NF)
            sp.dma_start(io["o_g"], GT[:, :, :]).then_inc(out_done, 16)
            sp.dma_start(io["o_cst"], io["state_conv"][:, 1, :]).then_inc(out_done, 16)
            sp.dma_start(io["o_fst"], io["state_ffn"][:, 1, :]).then_inc(out_done, 16)
            for m in range(KD):
                sp.wait_ge(d_px, 24 * (NF // 2 - 1) + NCH * (m + 1))
                sp.dma_start(io["y"][:, m, :], XT[:, m, :]).then_inc(out_done, 16)
            sp.wait_ge(out_done, 16 * (4 + KD))
            sp.wait_ge(k_saved, 16)
            sp.wait_ge(ki_saved, 16)
            sp.wait_ge(v_saved, 32)

        @block.tensor
        def _(pe):
            def proj(b, k, xh, xl, mid=None, extra=None, kn=KD):
                pe.wait_ge(w_lo[b], k + 1)
                if not (isinstance(k, int) and k == 0):
                    pe.wait_ge(ps_free[b], k)
                if extra:
                    extra()
                for c in range(NCH):
                    for kk in range(kn):
                        for p, (w, x) in enumerate(((WHI, xh), (WHI, xl), (WLO, xh))):
                            last = nc.tensor.matmul(PS[b][:, c, 0:CH], w[b][:, kk, :], x[:, kk, c * CH:(c + 1) * CH],
                                                    start=(kk == 0 and p == 0), stop=(kk == kn - 1 and p == 2))
                    if c == 0 and mid:
                        mid()
                last.then_inc(mm[b], 1)

            def norm_sums(acc, r, dst):
                pe.wait_ge(n_acc, (KD - 1) * (r + 1))
                for t in range(NB):
                    w = min(P, TP - t * P)
                    last = nc.tensor.matmul(PX[0][0:w, t:t + 1], acc[:, t * P:t * P + w], CK[:, C_ONES:C_ONES + 1],
                                            start=True, stop=True)
                last.then_inc(n_sum, 1)
                pe.wait_ge(n_rc, 2 * (r + 1))
                for t in range(NB):
                    w = min(P, TP - t * P)
                    last = nc.tensor.matmul(dst[:, t // 4, (t % 4) * P:(t % 4) * P + w],
                                            RT[0:w, t:t + 1].to_broadcast([w, P]), CK[0:w, C_ID:C_ID + w], start=True, stop=True)
                last.then_inc(n_bc, 1)

            def first_proj(b, k, r):
                pe.wait_ge(w_lo[b], k + 1)
                for kk in range(KD):
                    pe.wait_ge((n_lop, n_lo)[kk % 2], 4 * r + kk // 2 + 1)
                    for c in range(NCH):
                        for p, (w, x) in enumerate(((WHI, XH), (WHI, XL), (WLO, XH))):
                            last = nc.tensor.matmul(PS[b][:, c, 0:CH], w[b][:, kk, :], x[:, kk, c * CH:(c + 1) * CH],
                                                    start=(kk == 0 and p == 0), stop=(kk == KD - 1 and p == 2))
                last.then_inc(mm[b], 1)

            pe.wait_ge(const_in, 16)
            norm_sums(ACC, 0, PS[1])
            first_proj(0, 0, 0)
            proj(1, 0, XH, XL, extra=lambda: pe.wait_ge(n_t, 8))

            def head_weights():
                pe.wait_ge(ps_free[0], 1)
                for t in range(NB):
                    w = min(P, TP - t * P)
                    last = nc.tensor.transpose(PX[t // 8][0:w, (t % 8) * 64:(t % 8) * 64 + 4],
                                               EV[0][64:68, t * P:t * P + w], CK[64:68, C_ID + 64:C_ID + 68])
                last.then_inc(wi_t, 1)

            proj(0, 1, XH, XL, head_weights)
            pe.wait_ge(i_lo, 6)
            pe.wait_ge(qs_pad, 4)
            u = 0
            for b in range(2, NB):
                for h in range(IH):
                    if u < 2:
                        pe.wait_ge(ps_free[u], 2 - u)
                    else:
                        pe.wait_ge(sc_relu, u - 1)
                    for c0 in range(0, S_W[b], 512):
                        w = min(512, S_W[b] - c0)
                        for p, keys in enumerate((KH2, KL2)):
                            last = nc.tensor.matmul(PS[u % 2][:, c0 // 512, 0:w], QS[h][:, b * P:(b + 1) * P],
                                                    keys[:, c0:c0 + w], start=(p == 0), stop=(p == 1))
                    last.then_inc(sc_mm, 1)
                    u += 1
            pe.wait_ge(kidx_in, 16 * NS * PAGES)
            pe.wait_ge(qz_c, 8)
            pe.wait_ge(sc_relu, u)
            pe.wait_ge(wi_c, 2)

            def decode_scores(s):
                pe.wait_ge(kip_c, s + 1)
                for par in range(2):
                    last = nc.tensor.matmul(PS[0][0:32, par, :], QZ[par * HD:(par + 1) * HD, s, :],
                                            KIP[s % 2][par * HD:(par + 1) * HD, :, :].rearrange("p q t -> p (q t)"),
                                            start=(s == 0), stop=(s == NS - 1))
                last.then_inc(di_mm, 1)

            for s in range(NS):
                if s >= 2:
                    pe.wait_ge(kip_c, s - 1)
                for q in range(4):
                    page = s * PAGES + 2 * q
                    last = nc.tensor.transpose(PX[s % 2][:, q * P:(q + 1) * P],
                                               KIDX[:, page:page + 2, :].rearrange("p a d -> p (a d)"), ident)
                last.then_inc(kip_t, 1)
                if s >= 1:
                    decode_scores(s - 1)
            decode_scores(NS - 1)
            pe.wait_ge(zz_c, 1)
            nc.tensor.transpose(PX[0][0:32, 0:LR], ZZ[:, :], CK[0:LR, C_ID:C_ID + LR]).then_inc(zz_t, 1)
            pe.wait_ge(wds_c, 1)
            pe.wait_ge(di_relu, 1)
            for c in range(2):
                last = nc.tensor.matmul(PS[1][0:LR, c, :], WDS[:, :], RD[:, c * 512:(c + 1) * 512], start=True, stop=True)
            last.then_inc(ds_mm, 1)
            ms_rows = [PX[0][0:16, 0:CH], PX[1][0:16, 0:CH], PX[0][32:48, 0:CH]]

            def head_sums(j, b, ready):
                def go():
                    pe.wait_ge(ps_free[b], ready)
                    for c in range(NCH):
                        last = nc.tensor.matmul(ms_rows[c], SELC[b][:, :], SQ[:, c * CH:(c + 1) * CH],
                                                start=isinstance(j, int) and j == 0, stop=True, skip_group_check=True)
                    last.then_inc(r_ms, 1)
                return go

            proj(1, 1, XH, XL, extra=lambda: pe.wait_ge(s8_c, 1))
            proj(0, 2, XH, XL, head_sums(0, 1, 2))
            with pe.Fori(1, 4) as i:
                proj(1, 1 + i, XH, XL, head_sums(2 * i - 1, 0, i + 2))
                proj(0, 2 + i, XH, XL, head_sums(2 * i, 1, i + 2))
            def v_turn(b, v, first):
                pe.wait_ge(ps_free[b], 6 + (v + 1) // 2)
                for q, (t0, nt) in enumerate(((0, 4), (4, 4), (8, 1))):
                    if not (first and q < 2):
                        pe.wait_ge(v_c, 3 * v + q - 1)
                    for t in range(t0, t0 + nt):
                        w = min(P, TP - t * P)
                        last = nc.tensor.transpose(PX[(3 * b + q + 1) % 2][0:w, (t - t0) * P:(t - t0 + 1) * P],
                                                   EV[b][:, t * P:t * P + w], ident)
                    last.then_inc(v_t, 1)

            proj(1, 5, XH, XL, head_sums(7, 0, 6))
            proj(0, 6, XH, XL)
            pe.wait_ge(r_rt, 3)
            v_turn(1, 0, True)
            v_turn(0, 1, False)
            proj(1, 6, XH, XL)
            proj(0, 7, XH, XL)
            v_turn(1, 2, False)
            v_turn(0, 3, False)
            pe.wait_ge(r_rc, 1)
            for j in range(8):
                b = (j + 1) % 2
                if j < 2:
                    pe.wait_ge(ps_free[b], 7 if b else 8)
                else:
                    pe.wait_ge(r_ev2, j - 1)
                for c in range(NCH):
                    last = nc.tensor.matmul(PS[b][:, c, 0:CH], SELT[:, j, :], RS[:, c * CH:(c + 1) * CH],
                                            start=True, stop=True)
                last.then_inc(r_bc, 1)
            pe.wait_ge(r_ev2, 8)
            with pe.Fori(0, 6) as i:
                proj(1, 7 + i, XH, XL)
                proj(0, 8 + i, XH, XL)
            pe.wait_ge(v_c, 12)
            pe.wait_ge(r_nrm, 8)
            for j in range(4):
                last = nc.tensor.transpose(PX[0][0:32, j * P:(j + 1) * P], QKT[:, 4 + j, 8 * P:8 * P + 32], ident)
            last.then_inc(q_t, 1)
            with pe.Fori(0, 8) as i:
                proj(1, 13 + i, XH, XL)
                proj(0, 14 + i, XH, XL)
            pe.wait_ge(ps_free[1], 21)
            pe.wait_ge(ps_free[0], 22)
            pe.wait_ge(q_c, 1)

            def qk(u, i):
                u, i = unit(u, i)
                b, e = UNITS[u]
                if b == 0:
                    pe.wait_ge(hd_lo, 6 * i + 3 * e + 3)
                pe.wait_ge(a_max, NU * i + u - 1 + FREE)
                if S_W[b] > 1024:
                    pe.wait_ge(a_o, NU * i + u - 1 + FREE)
                pe.sem_inc(held, 1)
                for c0 in range(0, S_W[b], 512):
                    w = min(512, S_W[b] - c0)
                    for p, keys in enumerate((HKH, HKL)):
                        last = nc.tensor.matmul(PS[u % 2][:, c0 // 512, 0:w], HQ[e][:, b * P:(b + 1) * P],
                                                keys[e][:, c0:c0 + w], start=(p == 0), stop=(p == 1))
                last.then_inc(a_qk, 1)

            def turn(u, i):
                u, i = unit(u, i)
                b, e = UNITS[u]
                pe.wait_ge(a_exp, NU * i + u + 1)
                for t, k0, nk in BATCHES[u]:
                    pe.wait_ge(a_td if t % 2 else a_ta, (NBAT // 2) * i + t // 2 + 1)
                    pe.sem_inc(held, 1)
                    for kt in range(k0, k0 + nk):
                        w = min(P, S_W[b] - kt * P)
                        last = nc.tensor.transpose(PX[t % 2][0:w, (kt - k0) * P:(kt - k0) * P + ROWS[b]],
                                                   PB[u % 2][0:ROWS[b], kt * P:kt * P + w], CK[0:ROWS[b], C_ID:C_ID + ROWS[b]])
                    last.then_inc(a_tm, 1)

            def pv(u, i):
                b, e = UNITS[u]
                t = BATCHES[u][-1][0]
                pe.wait_ge(a_ta, (NBAT // 2) * i + t // 2 + 2)
                pe.wait_ge(a_td, (NBAT // 2) * i + (t + 1) // 2 + 1)
                pe.wait_ge(a_o, NU * i + u - 1 + FREE)
                if KT_N[b] == NB:
                    pe.wait_ge(a_vl, i + 1)
                pe.sem_inc(held, 1)
                for kt in range(KT_N[b]):
                    w = min(P, S_W[b] - kt * P)
                    v = VLAST[:, e * HD:(e + 1) * HD] if kt == 8 else VT[0:w, kt, ds(i * P + e * HD, HD)]
                    last = nc.tensor.matmul(PS[u % 2][0:ROWS[b], 2, 256:320], PTB[u % 2][0:w, kt, 0:ROWS[b]], v,
                                            start=(kt == 0), stop=(kt == KT_N[b] - 1))
                last.then_inc(a_pv, 1)

            def attend(i, last):
                def more(u):
                    return u < NU or not last
                for u in range(NU):
                    wide = more(u + 2) and S_W[UNITS[(u + 2) % NU][0]] > 1024
                    if more(u + 2) and not wide:
                        qk(u + 2, i)
                    if more(u + 1):
                        turn(u + 1, i)
                    pv(u, i)
                    if wide:
                        qk(u + 2, i)

            pe.sem_inc(a_pv, FREE)
            pe.sem_inc(a_tm, NBAT)
            qk(0, 0)
            qk(1, 0)
            turn(0, 0)
            with pe.Fori(0, 3) as i:
                attend(i, False)
            attend(3, True)
            pe.wait_ge(a_o, 4 * NU + FREE)
            for c in range(NCH):
                w = min(512, TP - c * 512)
                last = nc.tensor.matmul(PS[0][0:64, c, 0:w], CK[0:LR, C_E24:C_E24 + 64],
                                        S[0:LR, S_OFF[8] + c * 512:S_OFF[8] + c * 512 + w], start=True, stop=True)
            last.then_inc(d_mr, 1)
            pe.wait_ge(k_red, 64)
            for p in range(PAGES):
                nc.tensor.transpose(PS[1][0:64, p // 4, (p % 4) * P:(p % 4 + 1) * P],
                                    LD[:, p, :, :].rearrange("p s h -> p (s h)"), ident)
            pe.wait_ge(qa_c, 8)
            for j in range(4):
                last = nc.tensor.matmul(PS[1][0:64, 2, 0:LR], QA[:, j, :], QKT[:, j, 8 * P:8 * P + LR],
                                        start=(j == 0), stop=(j == 3))
            last.then_inc(d_l, 1)
            pe.wait_ge(d_exp, 1)
            for g in range(2):
                for p in range(4 * g, 4 * g + 4):
                    last = nc.tensor.transpose(PX[g][:, (p % 4) * 64:(p % 4 + 1) * 64], PD[:, p * P:(p + 1) * P],
                                               CK[0:64, C_ID:C_ID + 64])
                if g == 1:
                    last = nc.tensor.transpose(PX[1][0:LR, 256:320], PD[:, 8 * P:8 * P + LR], CK[0:64, C_ID:C_ID + 64])
                last.then_inc(d_t, 1)
            pe.wait_ge(d_c, 3)
            nc.tensor.matmul(PS[0][0:64, 0, :], PTN[:, :], VT[0:LR, 8, :], start=True, stop=False)
            for s in range(NS):
                pe.wait_ge(ring_in[s % 2], 128 * (4 + s // 2 + 1))
                for p in range(PAGES):
                    last = nc.tensor.matmul(PS[0][0:64, 0, :], PZ[:, (p * NS + s) * 64:(p * NS + s + 1) * 64], RING[s % 2][:, p, :],
                                            start=False, stop=(s == NS - 1 and p == PAGES - 1))
                last.then_inc(v_pv, 1)
            pe.wait_ge(d_o, 1)
            for j in range(4):
                last = nc.tensor.matmul(PS[0][:, 1, 8 * j:8 * j + 8], OD[:, j * P:(j + 1) * P], CK[0:64, C_OH:C_OH + 8],
                                        start=True, stop=True)
            last.then_inc(d_at, 1)
            n = 0
            for t in range(NB):
                if n >= 2:
                    pe.wait_ge(at_l, n - 1)
                for j in range(4):
                    last = nc.tensor.transpose(PX[n % 2][:, j * P:j * P + ROWS[t]], AT[0:ROWS[t], t, j * P:(j + 1) * P],
                                               CK[0:ROWS[t], C_ID:C_ID + ROWS[t]])
                last.then_inc(at_t, 1)
                n += 1
            pe.wait_ge(at_l, NB + 1)
            pe.wait_ge(co_l, 4)

            def outs(b, k, m):
                pe.wait_ge(w_lo[b], k + 1)
                for q, (xh, xl) in enumerate(((AH, AL), (COH, COL))):
                    if m is not None:
                        pe.wait_ge((o_m0, o_m1)[q], m)
                    for c in range(NCH):
                        for kk in range(4):
                            for p, (w, x) in enumerate(((WHI, xh), (WHI, xl), (WLO, xh))):
                                last = nc.tensor.matmul(PS[q][:, c, 0:CH], w[b][:, 4 * q + kk, :], x[:, kk, c * CH:(c + 1) * CH],
                                                        start=(kk == 0 and p == 0), stop=(kk == 3 and p == 2))
                    last.then_inc(mm[b] if q else o_ps, 1)

            outs(1, 21, None)
            outs(0, 22, 1)
            with pe.Fori(1, 4) as i:
                outs(1, 21 + i, 2 * i)
                outs(0, 22 + i, 2 * i + 1)

            def plain(b, k, wait):
                pe.wait_ge(w_lo[b], k + 1)
                wait()
                for c in range(NCH):
                    for kk in range(KD):
                        for p, (w, x) in enumerate(((WHI, XH), (WHI, XL), (WLO, XH))):
                            last = nc.tensor.matmul(PS[b][:, c, 0:CH], w[b][:, kk, :], x[:, kk, c * CH:(c + 1) * CH],
                                                    start=(kk == 0 and p == 0), stop=(kk == KD - 1 and p == 2))
                last.then_inc(mm[b], 1)

            pe.wait_ge(o_lo, 8)
            plain(1, 25, lambda: pe.wait_ge(o_m1, 8))
            plain(0, 26, lambda: pe.wait_ge(o_m0, 8))
            with pe.Fori(1, 4) as i:
                plain(1, 25 + i, lambda: pe.wait_ge(h_out, 2 * i - 1))
                plain(0, 26 + i, lambda: pe.wait_ge(h_out, 2 * i))
            pe.wait_ge(h_out, 8)
            norm_sums(HACC, 1, PS[0])

            def down(i, first):
                pe.wait_ge(f_lo, 2 * i + 2)
                pe.wait_ge(d_lo, i + 1)
                q = 0
                for m in range(KD):
                    for c in range(NCH):
                        if not (first and q < 2):
                            pe.wait_ge(d_px, 24 * i + q - 1)
                        for a in range(2):
                            for p, (w, x) in enumerate(((DHI, FH), (DHI, FL), (DLO, FH))):
                                last = nc.tensor.matmul(PX[q % 2][:, 0:CH], w[:, a, m * P:(m + 1) * P],
                                                        x[:, a, c * CH:(c + 1) * CH], start=(a == 0 and p == 0),
                                                        stop=(a == 1 and p == 2))
                        last.then_inc(d_mm, 1)
                        q += 1

            K0 = N_UP // 2

            def mixer(i, down_of, down_first):
                for a in range(2):
                    if down_of is None and a == 0:
                        first_proj(1, K0, 1)
                        plain(0, K0 + 1, lambda: pe.wait_ge(n_t, 16))
                        continue
                    plain(1, K0 + 2 * i + a, lambda: pe.wait_ge(f_g, 2 * i + a))
                    plain(0, K0 + 1 + 2 * i + a, lambda: pe.wait_ge(f_a, 2 * i + a))
                    if a == 0 and down_of is not None:
                        down(down_of, down_first)

            mixer(0, None, False)
            mixer(1, 0, True)
            with pe.Fori(2, NF // 2) as i:
                mixer(i, i - 1, False)
            down(NF // 2 - 1, False)

        @block.scalar
        def _(act):
            steps = [0]

            def step(ins):
                steps[0] += 1
                ins.then_inc(act_step, 1)
                act.wait_ge(act_step, steps[0])

            def hi(b, k):
                act.wait_ge(w_raw[b], 16 * (k + 1))
                if not (isinstance(k, int) and k == 0):
                    act.wait_ge(mm[b], k)
                nc.scalar.copy(WHI[b][:, :, :], WRAW[b][:, :, :]).then_inc(w_hi[b], 1)

            def norm_squares(src, k, sq, acc, r):
                if k >= 3:
                    act.wait_ge(n_acc, (KD - 1) * r + k - 2)
                dst = acc if k == 0 else sq[k % 2]
                nc.scalar.activation(dst[:, :], src[:, k, :], ACT.Square).then_inc(n_sq, 1)

            def norm_rest(tmp, r):
                act.wait_ge(n_sum, r + 1)
                nc.scalar.activation(RT[:, 0:8], PX[0][:, 0:8], ACT.Sqrt, bias=eps, scale=1.0 / D).then_inc(n_rt, 1)
                nc.scalar.activation(RT[0:32, 8:9], PX[0][0:32, 8:9], ACT.Sqrt, bias=eps[0:32, :], scale=1.0 / D).then_inc(n_rt, 1)
                for k in range(KD):
                    act.wait_ge(n_t, KD * r + k + 1)
                    nc.scalar.copy(XH[:, k, :], tmp[k % 2][:, :]).then_inc(n_hi, 1)

            act.wait_ge(const_in, 16)
            for k in range(KD):
                act.wait_ge(x_in[k], 16)
                norm_squares(XT, k, EV, ACC, 0)
            hi(0, 0)
            norm_rest(ROT, 0)

            def swap(dst, src, done):
                for q in range(4):
                    nc.scalar.copy(dst[32 * q:32 * q + 32, :], src[32 * (q ^ 1):32 * (q ^ 1) + 32, :]).then_inc(done, 1)

            hi(1, 0)
            act.wait_ge(mm[0], 1)
            nc.scalar.copy(v3(EV[0][:, :]), ps_all[0]).then_inc(ps_free[0], 1)
            act.wait_ge(ps_free[0], 1)
            swap(ROT[0], EV[0], i_rot)
            hi(0, 1)
            act.wait_ge(i_out, 1)
            nc.scalar.copy(KH2[0:HD, :], KIO[:, :]).then_inc(i_hi, 1)
            nc.scalar.copy(KH2[HD:P, :], KIO[:, :]).then_inc(i_hi, 1)
            act.dma_start(io["o_ki"], KIO[:, :]).then_inc(ki_saved, 16)
            step(nc.scalar.mul(QZ[:, :, :].rearrange("p s c -> p (s c)"), CK[:, 0:256], 0.0))
            qzf = QZ[:, :, :].rearrange("p s c -> p (s c)")

            def query_heads(t, b):
                act.wait_ge(i_out, t + 2)
                for e in range(2):
                    rows = slice(e * HD, (e + 1) * HD)
                    nc.scalar.copy(QS[2 * t + e][rows, 0:TP], EV[b][rows, :]).then_inc(i_hi, 1)
                for half in range(2):
                    for e in range(2):
                        h = 2 * t + e
                        nc.scalar.copy(qzf[half * HD:(half + 1) * HD, h:h + 36 * 7 + 1:36],
                                       EV[b][e * HD:(e + 1) * HD, TPR:TPR + NS]).then_inc(qz_c, 1)

            act.wait_ge(mm[1], 1)
            nc.scalar.copy(v3(EV[1][:, :]), ps_all[1]).then_inc(ps_free[1], 1)
            act.wait_ge(ps_free[1], 1)
            swap(ROT[1], EV[1], i_rot)
            hi(1, 1)
            act.wait_ge(wi_t, 1)
            nc.scalar.mul(WI[:, 0:8, :], PX[0][:, :].rearrange("p (t c) -> p t c", c=64)[:, :, 0:4], 1.0 / 16).then_inc(wi_c, 1)
            nc.scalar.mul(WI[0:32, 8, :], PX[1][0:32, 0:4], 1.0 / 16).then_inc(wi_c, 1)
            query_heads(0, 1)
            act.wait_ge(mm[0], 2)
            nc.scalar.copy(v3(EV[0][:, :]), ps_all[0]).then_inc(ps_free[0], 1)
            act.wait_ge(ps_free[0], 2)
            swap(ROT[0], EV[0], i_rot)
            query_heads(1, 0)
            act.wait_ge(i_lo, 6)
            for u in range(4 * (NB - 2)):
                b = 2 + u // 4
                act.wait_ge(sc_mm, u + 1)
                if u >= 2:
                    act.wait_ge(sc_acc, u - 1)
                src = PS[u % 2][0:ROWS[b], :, :].rearrange("p c t -> p (c t)")[:, 0:S_W[b]]
                nc.scalar.activation(EV[u % 2][0:ROWS[b], 0:S_W[b]], src, ACT.Relu).then_inc(sc_relu, 1)
            for s in range(NS):
                act.wait_ge(kip_t, s + 1)
                if s >= 2:
                    act.wait_ge(di_mm, s - 1)
                nc.scalar.copy(KIP[s % 2][:, :, :].rearrange("p q t -> p (q t)"), PX[s % 2][:, :]).then_inc(kip_c, 1)
            act.wait_ge(di_mm, NS)
            for par in range(2):
                ins = nc.scalar.activation(RD[:, :].rearrange("p (q r t) -> p r q t", r=2, t=P)[:, par, :, :],
                                           PS[0][0:32, par, :].rearrange("p (q t) -> p q t", t=P), ACT.Relu)
            ins.then_inc(di_relu, 1)
            act.wait_ge(zz_t, 1)
            nc.scalar.copy(WDS[:, :], PX[0][0:32, 0:LR]).then_inc(wds_c, 1)

            def v_evac(b, k, v, wait):
                act.wait_ge(mm[b], k + 1)
                if wait:
                    act.wait_ge(v_t, 3 * (v - 1))
                nc.scalar.copy(v3(EV[b][:, :]), ps_all[b]).then_inc(ps_free[b], 1)

            def v_copy(b, v):
                for q, (t0, nt) in enumerate(((0, 4), (4, 4), (8, 1))):
                    act.wait_ge(v_t, 3 * v + q + 1)
                    px = PX[(3 * b + q + 1) % 2]
                    if q < 2:
                        src = px[:, :].rearrange("p (t d) -> p t d", t=4)
                        nc.scalar.copy(VT[:, t0:t0 + 4, v * P:(v + 1) * P], src).then_inc(v_c, 1)
                    else:
                        nc.scalar.copy(VT[0:32, 8, v * P:(v + 1) * P], px[0:32, 0:P]).then_inc(v_c, 1)

            def rope(b, k, j, first):
                act.wait_ge(mm[b], k + 1)
                if not first:
                    act.wait_ge(r_out, j - 1)
                nc.scalar.activation(v3(EV[b][:, :]), ps_all[b], ACT.Copy, scale=WV[:, ds(W_QK + j, 1)]).then_inc(r_ev, 1)
                if not (isinstance(j, int) and j == 0):
                    act.wait_ge(r_ms, j)
                nc.scalar.copy(SELC[b][:, :], CK[:, ds(C_SEL + 16 * j, 16)])
                nc.scalar.activation(v3(SQ[:, :]), ps_all[b], ACT.Square).then_inc(ps_free[b], 1)
                act.wait_ge(r_ev, j + 1)
                swap(ROT2[b], EV[b], r_rot)

            act.wait_ge(sc_acc, 4 * (NB - 2))
            act.wait_ge(wv_in, 16)
            hi(0, 2)
            rope(1, 1, 0, True)
            hi(1, 2)
            rope(0, 2, 1, True)
            with act.Fori(1, 4) as i:
                hi(0, 2 + i)
                rope(1, 1 + i, 2 * i, False)
                hi(1, 2 + i)
                rope(0, 2 + i, 2 * i + 1, False)
            act.wait_ge(r_ms, 8)
            for c, src in enumerate((PX[0][0:16, 0:CH], PX[1][0:16, 0:CH], PX[0][32:48, 0:CH])):
                nc.scalar.activation(RS[:, c * CH:(c + 1) * CH], src, ACT.Sqrt, bias=eps[0:16, :],
                                     scale=1.0 / HD).then_inc(r_rt, 1)
            act.wait_ge(r_out, 8)
            hi(0, 6)
            v_evac(1, 5, 0, False)
            hi(1, 6)
            v_evac(0, 6, 1, False)
            v_copy(1, 0)
            v_copy(0, 1)
            hi(0, 7)
            v_evac(1, 6, 2, True)
            hi(1, 7)
            v_evac(0, 7, 3, True)
            v_copy(1, 2)
            v_copy(0, 3)
            act.wait_ge(v_c, 12)
            act.dma_start(io["o_v"][0:8, :, :].rearrange("t p d -> p t d"), VT[:, 0:8, :]).then_inc(v_saved, 16)
            act.dma_start(io["o_v"][8, 0:32, :], VT[0:32, 8, :]).then_inc(v_saved, 16)

            act.wait_ge(v_t, 12)
            for j in range(8):
                act.wait_ge(r_bc, j + 1)
                if j >= 2:
                    act.wait_ge(r_nrm, j - 1)
                nc.scalar.copy(v3(EV[(j + 1) % 2][:, :]), ps_all[(j + 1) % 2]).then_inc(r_ev2, 1)
            act.wait_ge(r_nrm, 8)
            act.wait_ge(ki_saved, 16)

            def conv(i, first):
                for a in range(2):
                    for q in range(3):
                        t = 3 * a + q
                        b = (1 + t) % 2
                        k = 7 + 3 * i + (t + 1) // 2
                        hi(1 - b, k if b == 0 else k + 1)
                        act.wait_ge(mm[b], k + 1)
                        j = 2 * i + a
                        if not (first and a == 0):
                            if q < 2:
                                act.wait_ge(c_u, j)
                            else:
                                act.wait_ge(c_out, j)
                        dst = (EV[0], EV[1], CB)[q]
                        nc.scalar.copy(v3(dst[:, :]), ps_all[b]).then_inc(ps_free[b], 1)
                    act.wait_ge(c_u, j + 1)
                    if not (first and a == 0):
                        act.wait_ge(c_dma, 16 * j)
                    for w in range(3):
                        nc.scalar.activation(TC[w][:, :], U[:, w:w + TP], ACT.Copy,
                                             scale=WV[:, ds(W_CW + 3 * j + w, 1)]).then_inc(c_t, 1)
                    act.wait_ge(c_t, 4 * j + 3)
                    for w in range(2):
                        nc.scalar.activation(TC[w][:, TPR:T], WV[:, ds(W_CS + 16 * j + 8 * w, 8)], ACT.Copy,
                                             scale=WV[:, ds(W_CW + 3 * j + w, 1)])
                    nc.scalar.copy(UT[:, ds(j, 1), :].rearrange("p a t -> p (a t)"), U[:, TPR:TPR + 10]).then_inc(c_t, 1)

            for i in range(2):
                conv(i, i == 0)
            act.wait_ge(c_t, 16)
            act.dma_start(io["o_u"], UT[:, :, :]).then_inc(out_done, 16)

            act.wait_ge(c_u, 4)

            def gate(b, k, i, first, hk):
                if hk is not None:
                    hi(1 - b, hk)
                act.wait_ge(mm[b], k + 1)
                if not first:
                    act.wait_ge(g_dma[b], 16 * i)
                nc.scalar.activation(v3(EV[b][:, :]), ps_all[b], ACT.Sigmoid).then_inc(ps_free[b], 1)
                act.wait_ge(ps_free[b], k + 1)
                act.dma_start(gates_d[ds(2 * i + (1 - b), 1), :, :].rearrange("a p t -> p (a t)"), EV[b][:, :]).then_inc(g_dma[b], 16)

            def head_parts(i, e):
                rows = slice(e * HD, (e + 1) * HD)
                act.wait_ge(a_qk, NU * i + 9 * e - 9)
                act.sem_inc(held, 1)
                parts(i, e)

            def parts(i, e):
                rows = slice(e * HD, (e + 1) * HD)
                nc.scalar.copy(HQ[e][rows, 0:TP], QKT[rows, ds(4 + i, 1), :].rearrange("p a t -> p (a t)")).then_inc(hd_hi, 1)
                for half in range(2):
                    nc.scalar.copy(HKH[e][half * HD:(half + 1) * HD, :],
                                   QKT[rows, ds(i, 1), :].rearrange("p a t -> p (a t)")).then_inc(hd_hi, 1)

            gate(1, 13, 0, True, 14)
            gate(0, 14, 0, True, 14)
            act.wait_ge(c_dma, 64)
            act.wait_ge(q_t, 1)
            nc.scalar.copy(QTOK[:, :], PX[0][0:32, :]).then_inc(q_c, 1)
            act.wait_ge(q_c, 1)
            act.dma_start(q_d.rearrange("a (s d) -> (a s) d", s=NS), QTOK[NMETA:NMETA + NS, :]).then_inc(q_dma, 16)
            nc.scalar.mul(HQ[0][:, TP:NB * P], CK[:, 0:NB * P - TP], 0.0)
            parts(0, 0)
            with act.Fori(1, 7) as i:
                gate(1, 13 + i, i, False, 14 + i)
                gate(0, 14 + i, i, False, 14 + i)
            gate(1, 20, 7, False, 21)
            gate(0, 21, 7, False, None)

            act.wait_ge(g_dma[0], 128)
            act.wait_ge(g_dma[1], 128)
            act.wait_ge(mm[1], 21)
            nc.scalar.mul(HQ[1][:, TP:NB * P], CK[:, 0:NB * P - TP], 0.0)
            parts(0, 1)
            step(nc.scalar.mul(QA[:, :, :].rearrange("p j c -> p (j c)"), CK[:, 0:256], 0.0))
            for j in range(4):
                for e in range(2):
                    nc.scalar.copy(QA[e * HD:(e + 1) * HD, j, 2 * j + e:2 * j + e + 57:8],
                                   QKT[e * HD:(e + 1) * HD, 4 + j, TPR:T]).then_inc(qa_c, 1)

            def t_evac(u, i):
                b, e = UNITS[u]
                for t, k0, nk in BATCHES[u]:
                    if t % 2 == 0:
                        act.wait_ge(a_tm, NBAT * (i + 1) + t + 1)
                        act.wait_ge(a_pv, NU * i + u - 1 + FREE)
                        _t_copy(nc.scalar.copy, PTB[u % 2], PX[t % 2], k0, nk, S_W[b], ROWS[b], a_ta)

            def expo(u, i):
                u, i = unit(u, i)
                b, e = UNITS[u]
                act.wait_ge(a_nm, NU * i + u + 1)
                nc.scalar.activation(PB[u % 2][0:ROWS[b], 0:S_W[b]], PB[u % 2][0:ROWS[b], 0:S_W[b]], ACT.Exp,
                                     bias=SM[0:ROWS[b], 18 + u:19 + u], scale=HD ** -0.5,
                                     accum_out=SM[0:ROWS[b], 36 + u:37 + u]).then_inc(a_exp, 1)

            def attend(i, first, last):
                for u in range(NU):
                    more = u + 1 < NU or not last
                    wide = more and S_W[UNITS[(u + 1) % NU][0]] > 1024
                    if more and not wide:
                        expo(u + 1, i)
                    t_evac(u, i)
                    if wide:
                        expo(u + 1, i)
                    if u == 2:
                        act.wait_ge(a_pv, NU * i + FREE)
                        act.sem_inc(held, 1)
                        nc.scalar.copy(VLAST[:, :], VT[0:32, 8, ds(i * P, P)]).then_inc(a_vl, 1)
                        if not first:
                            head_parts(i, 1)
                    if u == 10 and not last:
                        head_parts(i + 1, 0)

            act.sem_inc(a_ta, 1)
            expo(0, 0)
            attend(0, True, False)
            with act.Fori(1, 3) as i:
                attend(i, False, False)
            attend(3, False, True)
            act.wait_ge(d_mr, 1)
            nc.scalar.copy(MREP[:, 0:1024].rearrange("p (c t) -> p c t", t=512), PS[0][0:64, 0:2, :]).then_inc(d_mrc, 1)
            nc.scalar.copy(MREP[:, 1024:TP], PS[0][0:64, 2, 0:TP - 1024]).then_inc(d_mrc, 1)
            act.wait_ge(d_p, 1)
            nc.scalar.activation(PD[:, 0:PAST + LR], PD[:, 0:PAST + LR], ACT.Exp, bias=SM[0:64, 56:57], scale=HD ** -0.5,
                                 accum_out=SM[0:64, 57:58]).then_inc(d_exp, 1)
            act.wait_ge(pool_ready, 2)
            for g in range(2):
                act.wait_ge(d_t, g + 1)
                for p in range(4 * g, 4 * g + 4):
                    diagonal = PZ[:, p * 512:p * 512 + 576].rearrange("p (s c) -> p s c", c=72)[:, :, 0:8]
                    ins = nc.scalar.copy(diagonal, PX[g][:, (p % 4) * 64:(p % 4 + 1) * 64].rearrange("p (s h) -> p s h", h=8))
                ins.then_inc(d_c, 1)
            nc.scalar.copy(PTN[:, :], PX[1][0:LR, 256:320]).then_inc(d_c, 1)
            hi(1, 21)
            act.wait_ge(v_pv, NS)
            act.wait_ge(k_saved, 16)
            act.wait_ge(v_saved, 32)
            for t in range(NB):
                act.wait_ge(at_t, t + 1)
                w = P if t < 8 else NMETA
                nc.scalar.copy(AH[:, :, t * P:t * P + w],
                               PX[t % 2][:, :].rearrange("p (j t) -> p j t", j=4)[:, :, 0:w]).then_inc(at_h, 1)
            act.wait_ge(d_at, 1)
            nc.scalar.copy(AH[:, :, TPR:T], PS[0][:, 1, 0:32].rearrange("p (j t) -> p j t", j=4)).then_inc(at_h, 1)
            nc.scalar.mul(AH[:, :, T:TP], CK[:, 0:32].rearrange("p (j t) -> p j t", j=4), 0.0).then_inc(at_h, 1)
            for j in range(4):
                act.wait_ge(co_in[j % 2], 16 * (j // 2 + 1))
                nc.scalar.copy(COH[:, j, :], CRAW[j % 2][:, :]).then_inc(co_h, 1)

            for m in range(8):
                hi(m % 2, 22 + m // 2)
                act.wait_ge(o_mix, m + 1)
                nc.scalar.copy(XH[:, m, :], MT[m % 2][:, :]).then_inc(o_hi, 1)
            for m in range(8):
                hi(m % 2, 26 + m // 2)
                act.wait_ge(h_out, m + 1)
                norm_squares(XT, m, HSQ, HACC, 1)
            norm_rest(HT_, 1)

            for b in range(2):
                step(nc.scalar.mul(G[b][:, 0:2], CK[:, 0:2], 0.0))
            K0 = N_UP // 2

            def gate_half(i, a, first):
                f = 2 * i + a
                act.wait_ge(mm[1], K0 + 1 + f)
                if not first:
                    act.wait_ge(f_cv, f - 1)
                    act.wait_ge(f_lo, f - 1)
                nc.scalar.copy(v3(G[a][:, 2:TP + 2]), ps_all[1]).then_inc(f_g, 1)
                act.wait_ge(f_g, f + 1)
                nc.scalar.copy(GT[:, ds(f, 1), :].rearrange("p a t -> p (a t)"), G[a][:, TPR:TPR + 10])
                nc.scalar.activation(TG[a][:, :], G[a][:, 0:TP], ACT.Copy,
                                     scale=WV[:, ds(W_FW + 3 * f, 1)]).then_inc(f_t0, 1)

            def silu(i, a):
                f = 2 * i + a
                act.wait_ge(f_cv, f + 1)
                nc.scalar.activation(TG[a][:, :], TG[a][:, :], ACT.Silu, bias=WV[:, ds(W_FB + f, 1)]).then_inc(f_si, 1)

            def fhi(i, a):
                f = 2 * i + a
                act.wait_ge(f_a, f + 1)
                nc.scalar.copy(FH[:, a, :], TG[a][:, :]).then_inc(f_hi, 1)

            def mixer(i, first, last):
                f = 2 * i
                hi(0, K0 + 1 + f)
                gate_half(i, 0, first)
                hi(1, K0 + 1 + f)
                silu(i, 0)
                hi(0, K0 + 2 + f)
                if not first:
                    act.wait_ge(d_mm, 24 * i)
                fhi(i, 0)
                act.wait_ge(d_raw, 16 * (i + 1))
                nc.scalar.copy(DHI[:, :, :], DRAW[:, :, :]).then_inc(d_hi, 1)
                gate_half(i, 1, first)
                if not last:
                    hi(1, K0 + 2 + f)
                silu(i, 1)
                fhi(i, 1)

            mixer(0, True, False)
            with act.Fori(1, NF // 2 - 1) as i:
                mixer(i, False, False)
            mixer(NF // 2 - 1, False, True)

        @block.gpsimd
        def _(pool):
            def lo(b, k):
                pool.wait_ge(w_hi[b], k + 1)
                nc.gpsimd.tensor_tensor(WLO[b][:, :, :], WRAW[b][:, :, :], WHI[b][:, :, :].bitcast(F32),
                                        ALU.subtract).then_inc(w_lo[b], 1)

            lo(0, 0)

            def norm_lows(tmp, r):
                for k in range(0, KD, 2):
                    pool.wait_ge(n_hi, KD * r + k + 1)
                    nc.gpsimd.tensor_tensor(XL[:, k, :], tmp[0][:, :], XH[:, k, :].bitcast(F32), ALU.subtract).then_inc(n_lop, 1)

            norm_lows(ROT, 0)
            pool.wait_ge(n_t, KD)
            for h in range(IH):
                nc.gpsimd.memset(QPAD[h], 0.0).then_inc(qs_pad, 1)
            pool.wait_ge(rope_in, 32)
            for t in range(3):
                lo((t + 1) % 2, (t + 1) // 2)
                pool.wait_ge(i_rot, 4 * t + 4)
                nc.gpsimd.tensor_tensor(ROT[t % 2][:, :], ROT[t % 2][:, :], SIN[:, :], ALU.mult).then_inc(i_sin, 1)
            pool.wait_ge(rope2_in, 48)
            pool.wait_ge(wds_c, 1)
            pool.wait_ge(kip_c, 8)

            def rope(b, j):
                pool.wait_ge(r_rot, 4 * j + 4)
                nc.gpsimd.tensor_tensor(ROT2[b][:, :], ROT2[b][:, :], SIN2[:, :], ALU.mult).then_inc(r_sin, 1)
                nc.gpsimd.tensor_tensor(EV[b][:, :], EV[b][:, :], COS2[:, :], ALU.mult).then_inc(r_cos, 1)
                pool.wait_ge(r_cos, j + 1)
                nc.gpsimd.tensor_tensor(QKT[:, ds(j, 1), :].rearrange("p a t -> p (a t)"), EV[b][:, :], ROT2[b][:, :],
                                        ALU.add).then_inc(r_out, 1)

            with pool.Fori(0, 4) as i:
                lo(0, 2 + i)
                rope(1, 2 * i)
                lo(1, 2 + i)
                rope(0, 2 * i + 1)
            lo(0, 6)
            lo(1, 6)
            lo(0, 7)
            lo(1, 7)
            for j in range(8):
                pool.wait_ge(r_ev2, j + 1)
                nc.gpsimd.tensor_tensor(QKT[:, j, :], QKT[:, j, :], EV[(j + 1) % 2][:, :], ALU.mult).then_inc(r_nrm, 1)
            pool.wait_ge(r_nrm, 8)
            pool.dma_start(io["o_k"], QKT[:, 0:4, :]).then_inc(k_saved, 16)
            pool.wait_ge(ds_mm, 1)
            pool.wait_ge(ki_saved, 16)
            nc.gpsimd.memset(U[:, 0:2], 0.0).then_inc(pool_step, 1)

            for i in range(2):
                for a in range(2):
                    j = 2 * i + a
                    for q in range(3):
                        t = 3 * a + q
                        b = (1 + t) % 2
                        k = 7 + 3 * i + (t + 1) // 2
                        lo(1 - b, k if b == 0 else k + 1)
                        if q == 1:
                            pool.wait_ge(ps_free[b], k + 1)
                            if j >= 1:
                                pool.wait_ge(c_t, 4 * j)
                            nc.gpsimd.tensor_tensor(U[:, 2:TP + 2], EV[0][:, :], EV[1][:, :], ALU.mult).then_inc(c_u, 1)
                    pool.wait_ge(c_t, 4 * j + 4)
                    st = 1 + 2 * j
                    nc.gpsimd.tensor_tensor(TC[0][:, :], TC[0][:, :], TC[1][:, :], ALU.add).then_inc(pool_step, 1)
                    pool.wait_ge(pool_step, st + 1)
                    nc.gpsimd.tensor_tensor(TC[0][:, :], TC[0][:, :], TC[2][:, :], ALU.add).then_inc(pool_step, 1)
                    pool.wait_ge(pool_step, st + 2)
                    pool.wait_ge(ps_free[b], k + 1)
                    nc.gpsimd.tensor_tensor(TC[0][:, :], TC[0][:, :], CB[:, :], ALU.mult).then_inc(c_out, 1)
                    pool.wait_ge(c_out, j + 1)
                    pool.dma_start(conv_d[j, :, :], TC[0][:, :]).then_inc(c_dma, 16)
            lo(0, 14)
            lo(1, 14)

            def head_lows(i, e):
                rows, other = slice(e * HD, (e + 1) * HD), slice((1 - e) * HD, (2 - e) * HD)
                pool.wait_ge(hd_hi, 6 * i + 3 * e + 3)
                pool.sem_inc(held, 1)
                nc.gpsimd.tensor_tensor(HQ[e][other, 0:TP], QKT[rows, ds(4 + i, 1), :].rearrange("p a t -> p (a t)"),
                                        HQ[e][rows, 0:TP].bitcast(F32), ALU.subtract).then_inc(hd_lo, 1)
                for half in range(2):
                    pool.wait_ge(hd_lo, 6 * i + 3 * e + 1 + half)
                    pool.sem_inc(held, 1)
                    nc.gpsimd.tensor_tensor(HKL[e][half * HD:(half + 1) * HD, :],
                                            QKT[rows, ds(i, 1), :].rearrange("p a t -> p (a t)"),
                                            HKH[e][rows, :].bitcast(F32), ALU.subtract).then_inc(hd_lo, 1)
                pool.wait_ge(hd_lo, 6 * i + 3 * e + 3)
                pool.sem_inc(held, 1)

            pool.wait_ge(w_lo[1], 15)
            head_lows(0, 0)
            with pool.Fori(1, 7) as i:
                lo(0, 14 + i)
                lo(1, 14 + i)
            lo(0, 21)

            def sample(s, b):
                pool.wait_ge(ring_in[b], 128 * s + 128)
                for p in range(PAGES):
                    nc.gpsimd.tensor_tensor(RING[b][:, p, :], RING[b][:, p, :],
                                            QB[:, ds(2 * s + b, 1), :].rearrange("p a d -> p (a d)"),
                                            ALU.mult).then_inc(k_prod, 1)

            pool.wait_ge(qb_in, 16)
            with pool.Fori(0, 3) as i:
                sample(i, 0)
                pool.wait_ge(k_prod, 16 * i + 8)
                head_lows(i, 1)
                sample(i, 1)
                pool.wait_ge(k_prod, 16 * i + 16)
                head_lows(i + 1, 0)
            sample(3, 0)
            pool.wait_ge(k_prod, 56)
            head_lows(3, 1)
            sample(3, 1)
            pool.wait_ge(a_o, 4 * NU + FREE)
            for g in range(2):
                nc.gpsimd.memset(PZ[:, 2080 * g:2080 * (g + 1)], 0.0).then_inc(pool_ready, 1)
            lo(1, 21)
            lo(0, 22)
            for n in range(N_O + 2, N_UP + 1):
                lo(n % 2, n // 2)
            norm_lows(HT_, 1)
            K0 = N_UP // 2

            def dlo(i):
                pool.wait_ge(d_hi, i + 1)
                nc.gpsimd.tensor_tensor(DLO[:, :, :], DRAW[:, :, :], DHI[:, :, :].bitcast(F32), ALU.subtract).then_inc(d_lo, 1)

            def mixer(i, last):
                lo(0, K0 + 1 + 2 * i)
                lo(1, K0 + 1 + 2 * i)
                lo(0, K0 + 2 + 2 * i)
                dlo(i)
                if not last:
                    lo(1, K0 + 2 + 2 * i)

            with pool.Fori(0, NF // 2 - 1) as i:
                mixer(i, False)
            mixer(NF // 2 - 1, True)

        @block.vector
        def _(dve):
            steps = [0]

            def step(ins):
                steps[0] += 1
                ins.then_inc(dve_step, 1)
                dve.wait_ge(dve_step, steps[0])

            def norm_add(k, sq, acc, r):
                if k == 0:
                    return
                dve.wait_ge(n_sq, KD * r + k + 1)
                if k >= 2:
                    dve.wait_ge(n_acc, (KD - 1) * r + k - 1)
                nc.vector.tensor_tensor(acc[:, :], acc[:, :], sq[k % 2][:, :], ALU.add).then_inc(n_acc, 1)

            def norm_rest(src, tmp, wcol, r, ps):
                dve.wait_ge(n_rt, 2 * (r + 1))
                nc.vector.reciprocal(RT[:, 0:8], RT[:, 0:8]).then_inc(n_rc, 1)
                nc.vector.reciprocal(RT[0:32, 8:9], RT[0:32, 8:9]).then_inc(n_rc, 1)
                dve.wait_ge(n_bc, r + 1)
                rms = ps[:, :, :].rearrange("p c t -> p (c t)")[:, 0:TP]
                for k in range(KD):
                    if k >= 2:
                        dve.wait_ge(*((n_lop, 4 * r + k // 2) if k % 2 == 0 else (n_lo, 4 * r + k // 2)))
                    nc.vector.scalar_tensor_tensor(out=tmp[k % 2][:, :], in0=src[:, k, :], scalar=WV[:, wcol + k:wcol + k + 1],
                                                   in1=rms, op0=ALU.mult, op1=ALU.mult).then_inc(n_t, 1)
                    if k % 2:
                        dve.wait_ge(n_hi, KD * r + k + 1)
                        nc.vector.tensor_tensor(XL[:, k, :], tmp[1][:, :], XH[:, k, :].bitcast(F32), ALU.subtract).then_inc(n_lo, 1)

            for k in range(KD):
                norm_add(k, EV, ACC, 0)
            dve.wait_ge(wv_in, 16)
            norm_rest(XT, ROT, W_AN, 0, PS[1])

            dve.wait_ge(rope_in, 32)

            def rope(b, t, out, rows):
                dve.wait_ge(i_rot, 4 * t + 4)
                nc.vector.tensor_tensor(EV[b][0:rows, :], EV[b][0:rows, :], COS[0:rows, :], ALU.mult).then_inc(i_cos, 1)
                dve.wait_ge(i_cos, t + 1)
                dve.wait_ge(i_sin, t + 1)
                nc.vector.tensor_tensor(out, EV[b][0:rows, :], ROT[b][0:rows, :], ALU.add).then_inc(i_out, 1)

            rope(0, 0, KIO[:, :], HD)
            dve.wait_ge(i_hi, 2)
            for half in range(2):
                nc.vector.tensor_tensor(KL2[half * HD:(half + 1) * HD, :], KIO[:, :], KH2[0:HD, :].bitcast(F32),
                                        ALU.subtract).then_inc(i_lo, 1)
            for t in range(2):
                b = (t + 1) % 2
                rope(b, t + 1, EV[b][:, :], P)
                for e in range(2):
                    rows, other = slice(e * HD, (e + 1) * HD), slice((1 - e) * HD, (2 - e) * HD)
                    dve.wait_ge(i_hi, 2 * t + e + 3)
                    nc.vector.tensor_tensor(QS[2 * t + e][other, 0:TP], EV[b][rows, :], QS[2 * t + e][rows, 0:TP].bitcast(F32),
                                            ALU.subtract).then_inc(i_lo, 1)
            dve.wait_ge(wi_c, 2)
            u = 0
            for b in range(2, NB):
                s = S[0:ROWS[b], S_OFF[b]:S_OFF[b] + S_W[b]]
                for h in range(IH):
                    dve.wait_ge(sc_relu, u + 1)
                    r = EV[u % 2][0:ROWS[b], 0:S_W[b]]
                    w = WI[0:ROWS[b], b, h:h + 1]
                    if h == 0:
                        ins = nc.vector.tensor_scalar(s, r, w, 0.0, ALU.mult, ALU.add)
                    else:
                        ins = nc.vector.scalar_tensor_tensor(out=s, in0=r, scalar=w, in1=s, op0=ALU.mult, op1=ALU.add)
                    ins.then_inc(sc_acc, 1)
                    dve.wait_ge(sc_acc, u + 1)
                    u += 1
                if b < 8:
                    d = S[:, S_OFF[b] + b * P:S_OFF[b] + (b + 1) * P]
                    step(nc.vector.tensor_tensor(d, d, CK[:, C_CM:C_CM + P], ALU.add))
            nc.vector.tensor_tensor(ZZ[:, :].rearrange("p (s h) -> p s h", h=4),
                                    CK[0:LR, C_ZP:C_ZP + 32].rearrange("p (s h) -> p s h", h=4),
                                    WI[0:LR, 8:9, :].to_broadcast([LR, 8, 4]), ALU.mult).then_inc(zz_c, 1)
            s8 = S_OFF[8]
            step(nc.vector.tensor_tensor(SM[0:LR, 0:8], S[0:LR, s8 + TPR:s8 + T], CK[0:LR, C_DIAG:C_DIAG + 8], ALU.mult))
            step(nc.vector.reduce_sum(SM[0:LR, 8:9], SM[0:LR, 0:8], AX.X))
            step(nc.vector.tensor_scalar(S[0:LR, s8:s8 + TP], S[0:LR, s8:s8 + TP], CK[0:LR, C_ROWP:C_ROWP + 1], None, ALU.mult))
            step(nc.vector.tensor_tensor(S[0:LR, s8 + 1024:s8 + 1025], S[0:LR, s8 + 1024:s8 + 1025], SM[0:LR, 8:9], ALU.add))
            step(nc.vector.tensor_tensor(S[0:LR, s8 + 1024:s8 + TP], S[0:LR, s8 + 1024:s8 + TP], CK[0:LR, C_CM8:C_CM8 + 32], ALU.add))
            dve.wait_ge(ds_mm, 1)
            s8v = S[0:LR, s8:s8 + 1024].rearrange("p (c t) -> p c t", t=512)
            nc.vector.tensor_tensor(s8v, s8v, PS[1][0:LR, 0:2, :], ALU.add).then_inc(s8_c, 1)
            dve.wait_ge(s8_c, 1)
            def topk(blocks):
                base = steps[0]
                n = len(blocks)
                last = {}
                for _ in range(TOPK // 8):
                    for what in range(2):
                        for x, b in enumerate(blocks):
                            s = S[0:ROWS[b], S_OFF[b]:S_OFF[b] + S_W[b]]
                            if x in last:
                                dve.wait_ge(dve_step, last[x])
                            if what == 0:
                                ins = nc.vector.max(M8[x][0:ROWS[b], :], s)
                            else:
                                ins = nc.vector.match_replace(s, M8[x][0:ROWS[b], :], s, TAKEN)
                            ins.then_inc(dve_step, 1)
                            steps[0] += 1
                            last[x] = steps[0]
                dve.wait_ge(dve_step, steps[0])

            topk([7, 2])
            dve.wait_ge(r_rt, 3)
            nc.vector.reciprocal(RS[:, :], RS[:, :]).then_inc(r_rc, 1)
            topk([6, 3])
            topk([5, 4])
            topk([8])
            for b in range(2, NB):
                s = S[0:ROWS[b], S_OFF[b]:S_OFF[b] + S_W[b]]
                ins = nc.vector.tensor_scalar(s, s, 0.5 * TAKEN, NEG, ALU.is_gt, ALU.mult)
            ins.then_inc(masks_made, 1)

            def logits(u, i):
                u, i = unit(u, i)
                b, e = UNITS[u]
                r, w = ROWS[b], S_W[b]
                dve.wait_ge(a_qk, NU * i + u + 1)
                before = BATCHES[(u - 2) % NU][-1][0] + 1
                dve.wait_ge(a_tm, NBAT * (i + 1) + before if u >= 2 else NBAT * i + before)
                dve.sem_inc(held, 1)
                if b < 2:
                    if b == 1:
                        nc.vector.tensor_copy(PB[u % 2][:, 0:P], PS[u % 2][:, 0, 0:P])
                    nc.vector.tensor_tensor(PB[u % 2][:, b * P:w], PS[u % 2][:, 0, b * P:w], CK[:, C_CM:C_CM + P],
                                            ALU.add).then_inc(a_lg, 1)
                    dve.wait_ge(a_lg, 4 * i + 2 * e + b + 1)
                    nc.vector.reduce_max(SM[:, u:u + 1], PB[u % 2][:, 0:w], AX.X).then_inc(a_max, 1)
                else:
                    flat = PS[u % 2][0:r, :, :].rearrange("p c t -> p (c t)")[:, 0:w]
                    nc.vector.tensor_tensor_reduce(PB[u % 2][0:r, 0:w], flat, S[0:r, S_OFF[b]:S_OFF[b] + w], 1.0, -3.0e38,
                                                   ALU.add, ALU.max, SM[0:r, u:u + 1]).then_inc(a_max, 1)
                dve.wait_ge(a_max, NU * i + u + 1 + FREE)
                nc.vector.tensor_scalar(SM[0:r, 18 + u:19 + u], SM[0:r, u:u + 1], -(HD ** -0.5), None, ALU.mult).then_inc(a_nm, 1)

            def t_evac(u, i):
                b, e = UNITS[u]
                for t, k0, nk in BATCHES[u]:
                    if t % 2 == 1:
                        dve.wait_ge(a_tm, NBAT * (i + 1) + t + 1)
                        dve.wait_ge(a_pv, NU * i + u - 1 + FREE)
                        _t_copy(nc.vector.tensor_copy, PTB[u % 2], PX[t % 2], k0, nk, S_W[b], ROWS[b], a_td)

            def out(u, i):
                b, e = UNITS[u]
                r = ROWS[b]
                dve.wait_ge(a_exp, NU * i + u + 1)
                nc.vector.reciprocal(SM[0:r, 36 + u:37 + u], SM[0:r, 36 + u:37 + u]).then_inc(a_rc, 1)
                dve.wait_ge(a_rc, NU * i + u + 1)
                dve.wait_ge(a_pv, NU * i + u + 1 + FREE)
                nc.vector.tensor_scalar(AT[0:r, b, ds(i * P + e * HD, HD)], PS[u % 2][0:r, 2, 256:320],
                                        SM[0:r, 36 + u:37 + u], None, ALU.mult).then_inc(a_o, 1)

            def reduce_page(u, i):
                g = u - 2
                b, p = g // PAGES, g % PAGES
                dve.wait_ge(k_prod, 16 * i + g + 1)
                nc.vector.reduce_sum(LD[:, p, ds(2 * i + b, 1), :].rearrange("p a h -> p (a h)"),
                                     RING[b][:, p, :].rearrange("p (h d) -> p h d", d=HD), AX.X).then_inc(k_red, 1)

            def attend(i, last):
                for u in range(NU):
                    more = u + 1 < NU or not last
                    wide = more and S_W[UNITS[(u + 1) % NU][0]] > 1024
                    if more and not wide:
                        logits(u + 1, i)
                    t_evac(u, i)
                    if wide:
                        out(u - 1, i)
                        logits(u + 1, i)
                    if u >= 2:
                        reduce_page(u, i)
                    if u >= 1 and not wide:
                        out(u - 1, i)
                out(NU - 1, i)

            dve.wait_ge(g_dma[0], 128)
            dve.wait_ge(g_dma[1], 128)
            for s, n in ((a_max, FREE), (a_o, FREE), (a_td, 1)):
                dve.sem_inc(s, n)
            logits(0, 0)
            with dve.Fori(0, 3) as i:
                attend(i, False)
            attend(3, True)
            dve.wait_ge(d_mrc, 2)
            new = SM[0:64, 55:56]
            step(nc.vector.tensor_copy(new, MREP[:, 1024:1025]))
            step(nc.vector.tensor_scalar(MREP[:, 1024:1024 + LR], CK[0:64, C_NM:C_NM + LR], new, None, ALU.add))
            dve.wait_ge(d_l, 1)
            step(nc.vector.tensor_tensor_reduce(PD[:, 0:PAST + LR], PS[1][0:64, :, :].rearrange("p c t -> p (c t)")[:, 0:PAST + LR],
                                                MREP[:, 0:PAST + LR], 1.0, -3.0e38, ALU.add, ALU.max, SM[0:64, 54:55]))
            nc.vector.tensor_scalar(SM[0:64, 56:57], SM[0:64, 54:55], -(HD ** -0.5), None, ALU.mult).then_inc(d_p, 1)
            dve.wait_ge(d_exp, 1)
            step(nc.vector.reciprocal(SM[0:64, 58:59], SM[0:64, 57:58]))
            dve.wait_ge(v_pv, NS)
            nc.vector.scalar_tensor_tensor(out=OD[:, :], in0=PS[0][0:64, 0, :], scalar=SM[0:64, 58:59],
                                           in1=CK[0:64, C_BD:C_BD + 512], op0=ALU.mult, op1=ALU.mult).then_inc(d_o, 1)
            for t in range(NB):
                dve.wait_ge(at_h, t + 1)
                w = P if t < 8 else NMETA
                nc.vector.tensor_tensor(AL[:, :, t * P:t * P + w], PX[t % 2][:, :].rearrange("p (j t) -> p j t", j=4)[:, :, 0:w],
                                        AH[:, :, t * P:t * P + w].bitcast(F32), ALU.subtract).then_inc(at_l, 1)
            dve.wait_ge(at_h, NB + 2)
            step(nc.vector.tensor_tensor(AL[:, :, TPR:T], PS[0][:, 1, 0:32].rearrange("p (j t) -> p j t", j=4),
                                         AH[:, :, TPR:T].bitcast(F32), ALU.subtract))
            nc.vector.tensor_copy(AL[:, :, T:TP], AH[:, :, T:TP].bitcast(F32)).then_inc(at_l, 1)
            for j in range(4):
                dve.wait_ge(co_h, j + 1)
                nc.vector.tensor_tensor(COL[:, j, :], CRAW[j % 2][:, :], COH[:, j, :].bitcast(F32), ALU.subtract).then_inc(co_l, 1)
            for m in range(8):
                b = m % 2
                dve.wait_ge(o_ps, m + 1)
                dve.wait_ge(sg_in[b], 32 * (m // 2 + 1))
                if m >= 2:
                    dve.wait_ge(o_lo, m - 1)
                nc.vector.tensor_tensor(v3(MT[b][:, :]), v3(SGA[b][:, :]), ps_all[0], ALU.mult).then_inc(o_m0, 1)
                dve.wait_ge(mm[1 - b], 22 + m // 2 + b)
                nc.vector.tensor_tensor(v3(SGC[b][:, :]), v3(SGC[b][:, :]), ps_all[1], ALU.mult).then_inc(o_m1, 1)
                dve.wait_ge(o_m1, m + 1)
                nc.vector.tensor_tensor(MT[b][:, :], MT[b][:, :], SGC[b][:, :], ALU.add).then_inc(o_mix, 1)
                dve.wait_ge(o_hi, m + 1)
                nc.vector.tensor_tensor(XL[:, m, :], MT[b][:, :], XH[:, m, :].bitcast(F32), ALU.subtract).then_inc(o_lo, 1)
            for m in range(8):
                b = (N_MERGE + m) % 2
                dve.wait_ge(mm[b], (N_MERGE + m) // 2 + 1)
                dve.wait_ge(xr_in[m % 2], 16 * (m // 2 + 1))
                nc.vector.tensor_tensor(v3(XT[:, m, :]), v3(XR[m % 2][:, :]), ps_all[b], ALU.add).then_inc(h_out, 1)
                norm_add(m, HSQ, HACC, 1)
            norm_rest(XT, HT_, W_FN, 1, PS[0])

            K0 = N_UP // 2

            def conv(i, a):
                f = 2 * i + a
                w = [WV[:, ds(W_FW + 3 * f + q, 1)] for q in range(3)]
                dve.wait_ge(f_t0, f + 1)
                nc.vector.scalar_tensor_tensor(out=TG[a][:, :], in0=G[a][:, 1:TP + 1], scalar=w[1], in1=TG[a][:, :],
                                               op0=ALU.mult, op1=ALU.add).then_inc(f_s, 1)
                dve.wait_ge(f_s, 4 * f + 1)
                nc.vector.scalar_tensor_tensor(out=TG[a][:, :], in0=G[a][:, 2:TP + 2], scalar=w[2], in1=TG[a][:, :],
                                               op0=ALU.mult, op1=ALU.add).then_inc(f_s, 1)
                dve.wait_ge(f_s, 4 * f + 2)
                d = TG[a][:, TPR:T]
                nc.vector.tensor_scalar(d, WV[:, ds(W_FS + 16 * f, 8)], w[0], None, ALU.mult).then_inc(f_s, 1)
                dve.wait_ge(f_s, 4 * f + 3)
                nc.vector.scalar_tensor_tensor(out=d, in0=WV[:, ds(W_FS + 16 * f + 8, 8)], scalar=w[1], in1=d,
                                               op0=ALU.mult, op1=ALU.add).then_inc(f_s, 1)
                dve.wait_ge(f_s, 4 * f + 4)
                nc.vector.scalar_tensor_tensor(out=d, in0=G[a][:, TPR + 2:T + 2], scalar=w[2], in1=d,
                                               op0=ALU.mult, op1=ALU.add).then_inc(f_cv, 1)

            def times_val(i, a):
                f = 2 * i + a
                dve.wait_ge(f_si, f + 1)
                dve.wait_ge(mm[0], K0 + 2 + f)
                nc.vector.tensor_tensor(v3(TG[a][:, :]), v3(TG[a][:, :]), ps_all[0], ALU.mult).then_inc(f_a, 1)

            def flo(i, a):
                f = 2 * i + a
                dve.wait_ge(f_hi, f + 1)
                nc.vector.tensor_tensor(FL[:, a, :], TG[a][:, :], FH[:, a, :].bitcast(F32), ALU.subtract).then_inc(f_lo, 1)

            def down(i):
                q = 0
                for m in range(KD):
                    for c in range(NCH):
                        dve.wait_ge(d_mm, 24 * i + q + 1)
                        h = XT[:, m, c * CH:(c + 1) * CH]
                        nc.vector.tensor_tensor(h, h, PX[q % 2][:, 0:CH], ALU.add).then_inc(d_px, 1)
                        q += 1

            def mixer(i, first):
                conv(i, 0)
                times_val(i, 0)
                if not first:
                    down(i - 1)
                flo(i, 0)
                conv(i, 1)
                times_val(i, 1)
                flo(i, 1)

            mixer(0, True)
            with dve.Fori(1, NF // 2) as i:
                mixer(i, False)
            down(NF // 2 - 1)


def _constants():
    pos = np.concatenate([np.arange(TPR), np.full(TP - TPR, PAST)]).astype(np.float32)
    freqs = (10000.0 ** (-np.arange(32, dtype=np.float64) / 32)).astype(np.float32)
    ang = (pos[None, :] * freqs[:, None]).astype(np.float32)
    cos, sin = np.cos(ang), np.sin(ang)
    cos = np.concatenate([cos, cos, cos, cos]).astype(np.float32)
    sin = np.concatenate([-sin, sin, -sin, sin]).astype(np.float32)
    ck = np.zeros((P, C_END), np.float32)
    ck[:, C_ID:C_ID + P] = np.eye(P)
    ck[:, C_ONES:C_ONES + P] = 1.0
    r = np.arange(P)
    ck[:, C_CM:C_CM + P] = np.where(r[None, :] <= r[:, None], 0.0, NEG)
    for s in range(NS):
        ck[16 + s, C_E24 + 8 * s:C_E24 + 8 * s + 8] = 1.0
        ck[8 * s:8 * s + 8, C_OH + s] = 1.0
        ck[16 + s, C_DIAG + s] = 1.0
        ck[16 + s, C_ZP + 4 * s:C_ZP + 4 * s + 4] = 1.0
    ck[0:64, C_NM:C_NM + LR] = NEG
    for s in range(NS):
        for h in range(NH):
            ck[8 * s + h, C_BD + HD * h:C_BD + HD * (h + 1)] = 1.0
            ck[8 * s + h, C_NM + 16 + s] = 0.0
    ck[0:16, C_ROWP] = 1.0
    ck[:, C_EPS] = EPS
    ck[0:LR, C_CM8:C_CM8 + 32] = NEG
    for q in range(16):
        ck[q, C_CM8:C_CM8 + q + 1] = 0.0
    ck[16:LR, C_CM8] = 0.0
    selt = np.zeros((16, 8, P), np.float32)
    for j in range(8):
        ck[0:64, C_SEL + 16 * j + 2 * j] = 1.0
        ck[64:128, C_SEL + 16 * j + 2 * j + 1] = 1.0
        selt[2 * j, j, 0:64] = 1.0
        selt[2 * j + 1, j, 64:128] = 1.0
    return cos, sin, ck, selt


def _column_tiles(w, starts):
    k = w.shape[0] // P
    return np.stack([w[:, c:c + P].reshape(k, P, P).transpose(1, 0, 2).reshape(P, k * P) for c in starts])


def _by_feature(v, n):
    v = v.reshape(v.shape[:-1] + (n, P))
    return np.moveaxis(np.moveaxis(v, -1, 0), -1, 1)


def kernel(x_prompt, x_sample, cache_k, cache_v, cache_kidx, state_conv, state_ffn_conv, page_table,
           meta_tokens, attn_norm_w, w_in, q_norm_w, k_norm_w, conv_w, w_o_attn, w_o_conv, w_merge,
           ffn_norm_w, w_up, ffn_conv_w, ffn_conv_b, w_down):
    import concourse.bacc as bacc
    from concourse.bass_utils import run_bass_kernel_spmd

    f = np.float32
    x = np.concatenate([np.asarray(meta_tokens), np.asarray(x_prompt)[0], np.asarray(x_sample)[:, 0],
                        np.zeros((TP - T, D), f)])
    xt = np.ascontiguousarray(x.reshape(TP, KD, P).transpose(2, 1, 0))
    w_in = np.asarray(w_in)[0]
    q0, k0, v0, i0, ki0, cx0 = 0, 512, 1024, 1536, 1792, 1860
    cb0, cc0, ga0, gc0 = cx0 + 512, cx0 + 1024, cx0 + 1536, cx0 + 2560
    cols = [ki0, i0, i0 + P] + [k0 + P * j for j in range(4)] + [q0 + P * j for j in range(4)]
    cols += [v0 + P * j for j in range(4)]
    for j in range(4):
        cols += [cx0 + P * j, cc0 + P * j, cb0 + P * j]
    cols += [ga0 + P * j for j in range(8)] + [gc0 + P * j for j in range(8)]
    eight = [P * j for j in range(8)]
    w_up = np.asarray(w_up)[0]
    wtiles = np.concatenate([
        _column_tiles(w_in, cols),
        np.concatenate([_column_tiles(np.asarray(w_o_attn)[0], eight), _column_tiles(np.asarray(w_o_conv)[0], eight)], axis=2),
        _column_tiles(np.asarray(w_merge)[0], eight),
        _column_tiles(w_up, [P * (j // 2) + DFF * (j % 2) for j in range(2 * NF)]),
    ])
    wdown = np.asarray(w_down)[0].reshape(NF, P, D)
    qk = np.stack([np.tile(np.asarray(k_norm_w)[0], 2)] * 4 + [np.tile(np.asarray(q_norm_w)[0], 2)] * 4, axis=1)
    st_c, st_f = np.asarray(state_conv)[0], np.asarray(state_ffn_conv)[0]
    smallw = np.ascontiguousarray(np.concatenate([
        _by_feature(np.asarray(attn_norm_w)[0], 8), _by_feature(np.asarray(ffn_norm_w)[0], 8), qk,
        _by_feature(np.asarray(conv_w)[0], 4).reshape(P, -1),
        _by_feature(st_c.transpose(1, 0, 2), 4).reshape(P, -1),
        _by_feature(np.asarray(ffn_conv_w)[0], NF).reshape(P, -1),
        _by_feature(np.asarray(ffn_conv_b)[0], NF),
        _by_feature(st_f.transpose(1, 0, 2), NF).reshape(P, -1)], axis=1))
    cos, sin, ck, selt = _constants()
    n_phys = cache_k.shape[1]
    arrays = {
        "xT": xt, "wtiles": wtiles, "wdown": wdown, "smallw": smallw, "consts": ck, "cos": cos, "sin": sin, "selt": selt,
        "cache_k": np.asarray(cache_k)[0].reshape(n_phys, P, 512), "cache_v": np.asarray(cache_v)[0].reshape(n_phys, P, 512),
        "cache_kidx": np.asarray(cache_kidx)[0], "page_table": np.asarray(page_table).reshape(1, NS * PAGES),
        "state_conv": st_c, "state_ffn": st_f,
    }
    outs = {"y": (P, KD, TP), "o_k": (P, 4, TP), "o_v": (NB, P, 512), "o_ki": (HD, TP), "o_u": (P, 4, 10),
            "o_g": (P, NF, 10), "o_cst": (NS, 512), "o_fst": (NS, DFF)}
    nc = bacc.Bacc("TRN2", target_bir_lowering=False, num_devices=1)
    io = {}
    for name, a in arrays.items():
        a = arrays[name] = np.ascontiguousarray(a)
        io[name] = nc.dram_tensor(name, a.shape, mybir.dt.from_np(a.dtype), kind="ExternalInput").ap()
    for name, shape in outs.items():
        io[name] = nc.dram_tensor(name, shape, F32, kind="ExternalOutput").ap()
    build(nc, io)
    r = run_bass_kernel_spmd(nc, [arrays], core_ids=[0]).results[0]
    y = r["y"].transpose(2, 1, 0).reshape(TP, D)
    kk = r["o_k"].transpose(2, 1, 0).reshape(TP, NH, HD)
    vv = r["o_v"].reshape(NB * P, NH, HD)
    ki = r["o_ki"].transpose(1, 0)
    u = r["o_u"].transpose(2, 1, 0).reshape(10, 512)
    g = r["o_g"].transpose(2, 1, 0).reshape(10, DFF)
    return (y[NMETA:TPR][None], y[TPR:T][:, None],
            kk[None, None, :TPR], vv[None, None, :TPR], ki[None, None, :TPR], u[None, None, 0:2], g[None, None, 0:2],
            kk[TPR:T][None, :, None], vv[TPR:T][None, :, None], ki[TPR:T][None, :, None],
            np.stack([r["o_cst"], u[2:]], axis=1)[None], np.stack([r["o_fst"], g[2:]], axis=1)[None])
```

```python
from contextlib import ExitStack

import numpy as np

import concourse.bass as bass
from concourse import mybir

F32 = mybir.dt.float32
F32R = mybir.dt.float32r
I32 = mybir.dt.int32
ALU = mybir.AluOpType
ACT = mybir.ActivationFunctionType
AX = mybir.AxisListType
ds = bass.ds

P = 128
D = 1024
KD = D // P
NMETA = 16
TPR = 1040
NS = 8
T = TPR + NS
CH = 352
NCH = 3
TP = CH * NCH
NH, HD = 8, 64
IH = 4
NB = 9
LR = 24
PAGES = 8
PAST = PAGES * P
DFF = 2816
NF = DFF // P
TOPK = 256
EPS = 1e-6
NEG = -1.0e30
TAKEN = -3.0e38

N_KI, N_QI, N_KQ, N_V, N_CONV, N_GATE, N_O, N_MERGE, N_UP = 0, 1, 3, 11, 15, 27, 43, 51, 59
N_TILES = N_UP + 2 * NF

C_ID, C_ONES, C_CM, C_E24, C_OH, C_BD, C_NM, C_DIAG, C_ZP, C_ROWP, C_EPS, C_CM8 = (
    0, 128, 256, 384, 448, 456, 968, 992, 1000, 1032, 1033, 1034)
C_SEL = C_CM8 + 32
C_END = C_SEL + 128
W_AN, W_FN, W_QK, W_CW, W_CS, W_FW, W_FB, W_FS = 0, 8, 16, 24, 36, 100, 166, 188
W_END = W_FS + NF * 16

S_W = [P * (b + 1) for b in range(8)] + [TP]
S_OFF = {}
_o = 0
for _b in range(2, NB):
    S_OFF[_b] = _o
    _o += S_W[_b]
S_TOTAL = _o
ROWS = [P] * 8 + [LR]


def _t_copy(copy, dst, px, k0, nk, width, rows, done):
    if width - k0 * P >= nk * P:
        src = px[:, 0:nk * P].rearrange("p (t q) -> p t q", t=nk)[:, :, 0:rows]
        copy(dst[:, k0:k0 + nk, 0:rows], src).then_inc(done, 1)
    else:
        w = width - k0 * P
        copy(dst[0:w, k0, 0:rows], px[0:w, 0:rows]).then_inc(done, 1)


def build(nc, io):
    ctx = ExitStack()
    with ctx:
        base = -(-nc.sbuf_base // 32) * 32
        arena = ctx.enter_context(nc.sbuf_tensor("arena", [P, (nc.sbuf_usable_end - base) // 4 - 16], F32))

        def at(name, shape, off, dt=F32):
            n = 4
            for s in shape[1:]:
                n *= s
            assert base + off + n <= nc.sbuf_usable_end, (name, off, n)
            return nc.alloc_sbuf_tensor_at(name, shape, dt, offset=base + off)

        R = 4 * TP
        WRAW = [at(f"WRAW{b}", [P, KD, P], 4096 * b) for b in range(2)]
        WHI = [at(f"WHI{b}", [P, KD, P], 8192 + 4096 * b, F32R) for b in range(2)]
        WLO = [at(f"WLO{b}", [P, KD, P], 16384 + 4096 * b, F32R) for b in range(2)]
        o1 = 24576
        XT = at("XT", [P, KD, TP], o1)
        QKT = at("QKT", [P, 8, TP], o1)
        o2 = o1 + 8 * R
        VT = at("VT", [P, NB, 512], o2)
        o3 = o2 + NB * 2048
        ROT = [at(f"ROT{b}", [P, TP], o3 + b * R) for b in range(2)]
        COS = at("COS", [P, TP], o3 + 2 * R)
        SIN = at("SIN", [P, TP], o3 + 3 * R)
        ACC = at("ACC", [P, TP], o3 + 4 * R)
        S = at("S", [P, S_TOTAL], o3)
        SELT = at("SELT", [16, 8, P], o3 + 5 * R)
        o4 = o3 + 6 * R
        EV = [at(f"EV{b}", [P, TP], o4 + b * R) for b in range(2)]
        QS = [at(f"QS{h}", [P, NB * P], o1 + 4608 * h, F32R) for h in range(IH)]
        KH2 = at("KH2", [P, TP], o1 + 18432, F32R)
        KL2 = at("KL2", [P, TP], o1 + 18432 + R, F32R)
        KIP = [at(f"KIP{b}", [P, 4, P], o1 + 26880 + 2048 * b) for b in range(2)]
        QZ = at("QZ", [P, NS, 32], o1 + 30976)
        ZZ = at("ZZ", [LR, 32], o1 + 32000)
        WDS = at("WDS", [32, LR], o1 + 32128)
        RD = at("RD", [32, 1024], o2 + 2 * R)
        o5 = o4 + 2 * R
        KIDX = at("KIDX", [P, NS * PAGES, HD], o5)
        KIO = at("KIO", [HD, TP], o5 + 16384)
        COS2 = at("COS2", [P, TP], o2)
        SIN2 = at("SIN2", [P, TP], o2 + R)
        ROT2 = [at(f"ROT2{b}", [P, TP], o2 + (2 + b) * R) for b in range(2)]
        SQ = at("SQ", [P, TP], o5)
        RS = at("RS", [16, TP], o5 + R)
        CB = at("CB", [P, TP], o5)
        U = at("U", [P, TP + 2], o5 + R)
        TC = [at(f"TC{j}", [P, TP], o5 + 2 * R + 64 + j * R) for j in range(3)]
        o7 = 134080
        XH = at("XH", [P, KD, TP], o7, F32R)
        XL = at("XL", [P, KD, TP], o7 + 8 * R, F32R)
        oc = o7 + 16 * R
        CK = at("CK", [P, C_END], oc)
        WV = at("WV", [P, W_END], oc + 4800)
        om = oc + 4800 + 2176
        WI = at("WI", [P, NB, IH], om)
        UT = at("UT", [P, 4, 10], om + 160)
        GT = at("GT", [P, NF, 10], om + 320)
        PT = at("PT", [1, NS * PAGES], om + 1216, I32)
        SM = at("SM", [P, 64], om + 1472)
        M8 = [at(f"M8{j}", [P, 8], om + 1728 + 32 * j) for j in range(2)]
        SELC = [at(f"SELC{j}", [P, 16], om + 1792 + 64 * j) for j in range(2)]
        RT = at("RT", [P, NB], om + 1920)
        QPAD = [QS[h][:, TP:NB * P].bitcast(F32) for h in range(IH)]
        PB = [at(f"PB{b}", [P, TP], 97920 + b * R) for b in range(2)]
        PTB = [at(f"PTB{b}", [P, NB, P], 106368 + 4608 * b) for b in range(2)]
        oh = (115584, 0)
        HQ = [at(f"HQ{b}", [P, NB * P], oh[b], F32R) for b in range(2)]
        HKH = [at(f"HKH{b}", [P, TP], oh[b] + 4608, F32R) for b in range(2)]
        HKL = [at(f"HKL{b}", [P, TP], oh[b] + 4608 + R, F32R) for b in range(2)]
        LD = at("LD", [P, PAGES, NS, NH], 128640)
        QTOK = at("QTOK", [32, 512], 130688)
        VLAST = at("VLAST", [32, P], 132736)
        QA = at("QA", [P, 4, 64], 16384)
        RING = [at(f"RING{b}", [P, PAGES, 512], 133824 + 16384 * b) for b in range(2)]
        QB = at("QB", [P, NS, 512], 166592)
        AT = at("AT", [P, NB, 512], 183232)
        PZ = at("PZ", [P, PAGES * NS * 64 + 64], 166592)
        PD = at("PD", [64, TP], 17408)
        PTN = at("PTN", [LR, 64], 21632)
        OD = at("OD", [64, 512], 17408)
        AH = at("AH", [P, 4, TP], o1, F32R)
        AL = at("AL", [P, 4, TP], o1 + 4 * R, F32R)
        COH = at("COH", [P, 4, TP], o2, F32R)
        COL = at("COL", [P, 4, TP], o2 + 4 * R, F32R)
        og = o2 + 8 * R
        SGA = [at(f"SGA{b}", [P, TP], og + b * R) for b in range(2)]
        SGC = [at(f"SGC{b}", [P, TP], og + (2 + b) * R) for b in range(2)]
        MT = [at(f"MT{b}", [P, TP], og + (4 + b) * R) for b in range(2)]
        CRAW = [at(f"CRAW{b}", [P, TP], 115584 + b * R) for b in range(4)]
        XR = [at(f"XR{b}", [P, TP], o2 + b * R) for b in range(2)]
        HSQ = [at(f"HSQ{b}", [P, TP], o2 + (2 + b) * R) for b in range(2)]
        HACC = at("HACC", [P, TP], o2 + 4 * R)
        HT_ = [at(f"HT{b}", [P, TP], o2 + (5 + b) * R) for b in range(4)]
        FH = at("FH", [P, 2, TP], o2, F32R)
        FL = at("FL", [P, 2, TP], o2 + 2 * R, F32R)
        of = o2 + 4 * R
        DRAW = at("DRAW", [P, 2, D], of)
        DHI = at("DHI", [P, 2, D], of + 8192, F32R)
        DLO = at("DLO", [P, 2, D], of + 16384, F32R)
        G = [at(f"G{b}", [P, TP + 2], of + 24576 + 4256 * b) for b in range(2)]
        TG = [at(f"TG{b}", [P, TP], of + 33088 + R * b) for b in range(2)]
        assert of + 33088 + 2 * R <= 134080

        PS = [ctx.enter_context(nc.psum_tensor(f"PS{b}", [P, NCH, 512], F32)) for b in range(2)]
        PX = [ctx.enter_context(nc.psum_tensor(f"PX{b}", [P, 512], F32)) for b in range(2)]
        px_out = [t[:, 2, 32:32 + HD] for t in PS]
        at_banks = (PX[0], PX[1], PS[0][:, 0, :], PS[0][:, 2, :])
        px_dec = [t[0:64, 2, 96:352] for t in PS]
        ps_all = [t[:, :, 0:CH] for t in PS]

        def v3(ap):
            return ap.rearrange("p (c t) -> p c t", c=NCH)

        ident = CK[:, C_ID:C_ID + P]
        ones = CK[:, C_ONES:C_ONES + P]
        eps = CK[:, C_EPS:C_EPS + 1]

        xt_d, ws_d, wd_d = io["xT"], io["wtiles"], io["wdown"]
        gates_d = nc.dram_tensor("gates", (16, P, TP), F32, kind="Internal").ap()
        q_d = nc.dram_tensor("decode_q", (1, NS * 512), F32, kind="Internal").ap()
        conv_d = nc.dram_tensor("convout", (4, P, TP), F32, kind="Internal").ap()

        def sem(name):
            return ctx.enter_context(nc.semaphore(name))

        w_raw = [sem(f"w_raw{b}") for b in range(2)]
        w_hi = [sem(f"w_hi{b}") for b in range(2)]
        w_lo = [sem(f"w_lo{b}") for b in range(2)]
        mm = [sem(f"mm{b}") for b in range(2)]
        ps_free = [sem(f"ps_free{b}") for b in range(2)]
        const_in, wv_in, rope_in, pt_in = sem("const_in"), sem("wv_in"), sem("rope_in"), sem("pt_in")
        x_in = [sem(f"x_in{k}") for k in range(KD)]
        n_sq, n_acc, n_sum, n_rt, n_rc, n_bc, n_t, n_hi, n_lo, n_lop = (
            sem(s) for s in ("n_sq", "n_acc", "n_sum", "n_rt", "n_rc", "n_bc", "n_t", "n_hi", "n_lo", "n_lop"))
        i_rot, i_cos, i_sin, i_out, i_hi, i_lo, qs_pad = (
            sem(s) for s in ("i_rot", "i_cos", "i_sin", "i_out", "i_hi", "i_lo", "qs_pad"))
        r_ev, r_rot, r_cos, r_out, r_ms, r_rt, r_rc, r_bc, r_nrm = (
            sem(s) for s in ("r_ev", "r_rot", "r_cos", "r_out", "r_ms", "r_rt", "r_rc", "r_bc", "r_nrm"))
        act_step, dve_step, pool_step = sem("act_step"), sem("dve_step"), sem("pool_step")
        wi_t, wi_c = sem("wi_t"), sem("wi_c")
        rope2_in, r_ev2 = sem("rope2_in"), sem("r_ev2")
        sc_mm, sc_relu, sc_acc = sem("sc_mm"), sem("sc_relu"), sem("sc_acc")
        kidx_in = [sem(f"kidx_in{s}") for s in range(NS)]
        qz_c, kip_t, kip_c, di_mm, di_relu, zz_c, zz_t, wds_c, ds_mm, s8_c = (
            sem(s) for s in ("qz_c", "kip_t", "kip_c", "di_mm", "di_relu", "zz_c", "zz_t", "wds_c", "ds_mm", "s8_c"))
        v_t, v_c = sem("v_t"), sem("v_c")
        c_u, c_t, c_out = sem("c_u"), sem("c_t"), sem("c_out")
        c_dma = sem("c_dma")
        g_dma = [sem(f"g_dma{b}") for b in range(2)]
        held = sem("held")
        out_done, k_saved, ki_saved, v_saved = (sem(s) for s in ("out_done", "k_saved", "ki_saved", "v_saved"))
        q_t, q_c, q_dma, qb_in, qa_c, pool_ready = (
            sem(s) for s in ("q_t", "q_c", "q_dma", "qb_in", "qa_c", "pool_ready"))
        ring_in = [[sem(f"ring_in{b}{h}") for h in range(2)] for b in range(2)]
        qb_rest = sem("qb_rest")
        k_prod, k_red = sem("k_prod"), sem("k_red")
        hd_hi, hd_lo, a_vl, a_qk, a_lg, a_max, a_nm, a_exp, a_rc, a_tm, a_ta, a_pv, a_o = (
            sem(s) for s in ("hd_hi", "hd_lo", "a_vl", "a_qk", "a_lg", "a_max", "a_nm", "a_exp", "a_rc", "a_tm", "a_ta", "a_pv", "a_o"))
        d_l, d_p, d_exp, d_t, d_c, d_o, d_at, at_t, at_h, at_l = (
            sem(s) for s in ("d_l", "d_p", "d_exp", "d_t", "d_c", "d_o", "d_at", "at_t", "at_h", "at_l"))
        co_in = [sem(f"co_in{b}") for b in range(4)]
        co_h, co_l, co_lp = sem("co_h"), sem("co_l"), sem("co_lp")
        sg_in = [sem(f"sg_in{b}") for b in range(2)]
        o_ps, o_m0, o_m1, o_mix, o_hi, o_lo = (sem(s) for s in ("o_ps", "o_m0", "o_m1", "o_mix", "o_hi", "o_lo"))
        xr_in = [sem(f"xr_in{b}") for b in range(2)]
        h_out = sem("h_out")
        f_g, f_t0, f_s, f_cv, f_si, f_a, f_hi, f_lo = (sem(s) for s in ("f_g", "f_t0", "f_s", "f_cv", "f_si", "f_a", "f_hi", "f_lo"))
        d_raw, d_hi, d_lo, d_mm, d_px = sem("d_raw"), sem("d_hi"), sem("d_lo"), sem("d_mm"), sem("d_px")

        block = ctx.enter_context(nc.Block())

        ORDER = (0, 4, 3, 6, 1, 7, 2, 8, 5)
        UNITS = [(b, e) for e in range(2) for b in ORDER]
        FREE = 2
        NU = len(UNITS)
        KT_N = [-(-S_W[b] // P) for b in range(NB)]
        BATCHES = []
        _n = 0
        for b, e in UNITS:
            mine = []
            for k0 in range(0, KT_N[b], 4):
                mine.append((_n, k0, min(4, KT_N[b] - k0)))
                _n += 1
            BATCHES.append(mine)
        NBAT = _n
        assert NBAT % 2 == 0 and NU % 2 == 0

        def unit(u, i):
            return (u, i) if u < NU else (u - NU, i + 1)

        @block.sync
        def _(sp):
            sp.dma_start(PT[:, :], io["page_table"]).then_inc(pt_in, 16)
            sp.dma_start(CK[:, :], io["consts"]).then_inc(const_in, 16)
            for k in range(KD):
                sp.dma_start(XT[:, k, :], xt_d[:, k, :]).then_inc(x_in[k], 16)
            sp.dma_start(WV[:, :], io["smallw"]).then_inc(wv_in, 16)

            def load(n, b):
                sp.dma_start(WRAW[b][:, :, :].rearrange("p k m -> p (k m)"),
                             ws_d[ds(n, 1), :, :].rearrange("a p m -> p (a m)")).then_inc(w_raw[b], 16)

            load(0, 0)
            load(1, 1)
            sp.dma_start(COS[:, :], io["cos"]).then_inc(rope_in, 16)
            sp.dma_start(SIN[:, :], io["sin"]).then_inc(rope_in, 16)
            sp.wait_ge(pt_in, 16)

            def indexer_pages(s):
                with sp.Fori(s * PAGES, (s + 1) * PAGES) as j:
                    page = sp.value_load(PT[0:1, ds(j, 1)], min_val=0, max_val=79)
                    sp.dma_start(KIDX[:, ds(j, 1), :].rearrange("p a d -> p (a d)"),
                                 io["cache_kidx"][ds(page, 1), :, :].rearrange("a p d -> p (a d)")).then_inc(kidx_in[s], 16)

            for s in range(2):
                indexer_pages(s)
            sp.wait_ge(w_lo[0], 1)
            load(2, 0)
            for s in range(2, 4):
                indexer_pages(s)
            sp.wait_ge(w_lo[1], 1)
            load(3, 1)
            for s in range(4, NS):
                indexer_pages(s)
            sp.dma_start(COS2[:, :], io["cos"]).then_inc(rope2_in, 16)
            sp.dma_start(SIN2[:, :], io["sin"]).then_inc(rope2_in, 16)
            sp.dma_start(SELT[:, :, :], io["selt"]).then_inc(rope2_in, 16)

            def weights(n0, n1):
                with sp.Fori(n0 // 2, n1 // 2) as k:
                    for b in range(2):
                        sp.wait_ge(w_lo[b], k)
                        load(2 * k + b, b)

            weights(4, N_O - 1)
            sp.wait_ge(w_lo[0], 21)
            load(N_O - 1, 0)
            sp.wait_ge(mm[0], 22)
            sp.wait_ge(q_dma, 16)
            sp.wait_ge(g_dma[0], 128)

            def spread_queries(s0, s1, done):
                sp.dma_start(QB[:, s0:s1, :].rearrange("p s d -> p (s d)"),
                             q_d[:, s0 * 512:s1 * 512].to_broadcast([P, (s1 - s0) * 512])).then_inc(done, 16)

            spread_queries(0, 2, qb_in)

            def pages(cache, s, b, wait=None):
                for p in range(PAGES):
                    if wait and p % 4 == 0:
                        wait(p // 4)
                    page = sp.value_load(PT[0:1, ds(s * PAGES + p, 1)], min_val=0, max_val=79)
                    sp.dma_start(RING[b][:, p, :],
                                 cache[ds(page, 1), :, :].rearrange("a p d -> p (a d)")).then_inc(ring_in[b][p // 4], 16)

            pages(io["cache_k"], 0, 0)
            spread_queries(2, NS, qb_rest)
            pages(io["cache_k"], 1, 1)
            with sp.Fori(1, NS // 2) as i:
                for b in range(2):
                    pages(io["cache_k"], 2 * i + b, b, lambda h: sp.wait_ge(k_red, 8 * i + 4 * b - 6 + 2 * h))
            for b in range(2):
                pages(io["cache_v"], b, b, lambda h: sp.wait_ge(k_red, 26 + 4 * b + 2 * h))
            with sp.Fori(1, NS // 2) as i:
                for b in range(2):
                    pages(io["cache_v"], 2 * i + b, b,
                          lambda h: sp.wait_ge(a_pv, 2 * NU + 4 + FREE + 9 * (i - 1) + 4 * b + 2 * h))
            sp.wait_ge(c_dma, 64)
            sp.wait_ge(a_qk, 3 * NU + NB)
            for j in range(4):
                sp.dma_start(CRAW[j][:, :], conv_d[j, :, :]).then_inc(co_in[j], 16)
            sp.wait_ge(a_qk, 4 * NU)
            load(N_O, 1)
            load(N_O + 1, 0)
            sp.wait_ge(a_o, 4 * NU + FREE)
            for b in range(2):
                sp.wait_ge(g_dma[b], 128)

            def load_next(n, b, k):
                sp.wait_ge(w_lo[b], k)
                load(n, b)

            def out_tiles(m, a, first):
                if not first:
                    sp.wait_ge(o_mix, m + a - 1)
                sp.dma_start(SGA[a][:, :], gates_d[ds(m + a, 1), :, :].rearrange("a p t -> p (a t)")).then_inc(sg_in[a], 16)
                sp.dma_start(SGC[a][:, :], gates_d[ds(m + a + 8, 1), :, :].rearrange("a p t -> p (a t)")).then_inc(sg_in[a], 16)

            for a in range(2):
                out_tiles(0, a, True)
                load_next(N_O + 2 + a, 1 - a, 22 + a)
            with sp.Fori(1, 4) as i:
                for a in range(2):
                    out_tiles(2 * i, a, False)
                    load_next(N_O + 2 + 2 * i + a, 1 - a, 22 + i + a)
            sp.wait_ge(mm[0], 26)
            for a in range(2):
                sp.dma_start(XR[a][:, :], xt_d[:, a, :]).then_inc(xr_in[a], 16)
                load_next(N_MERGE + 2 + a, 1 - a, 26 + a)
            with sp.Fori(1, 4) as i:
                for a in range(2):
                    sp.wait_ge(h_out, 2 * i + a - 1)
                    sp.dma_start(XR[a][:, :], xt_d[:, ds(2 * i + a, 1), :].rearrange("p a t -> p (a t)")).then_inc(xr_in[a], 16)
                    load_next(N_MERGE + 2 + 2 * i + a, 1 - a, 26 + i + a)
            sp.wait_ge(n_lo, 8)
            sp.wait_ge(n_lop, 8)

            def mixer(i, first, last):
                if not first:
                    sp.wait_ge(d_lo, i)
                sp.dma_start(DRAW[:, :, :], wd_d[ds(2 * i, 2), :, :].rearrange("a p m -> p a m")).then_inc(d_raw, 16)
                for q in range(2 if last else 4):
                    load_next(N_UP + 2 + 4 * i + q, 1 - q % 2, 30 + 2 * i + (q + 1) // 2)

            mixer(0, True, False)
            with sp.Fori(1, NF // 2 - 1) as i:
                mixer(i, False, False)
            mixer(NF // 2 - 1, False, True)
            sp.wait_ge(f_t0, NF)
            sp.dma_start(io["o_g"], GT[:, :, :]).then_inc(out_done, 16)
            sp.dma_start(io["o_cst"], io["state_conv"][:, 1, :]).then_inc(out_done, 16)
            sp.dma_start(io["o_fst"], io["state_ffn"][:, 1, :]).then_inc(out_done, 16)
            for m in range(KD):
                sp.wait_ge(d_px, 24 * (NF // 2 - 1) + NCH * (m + 1))
                sp.dma_start(io["y"][:, m, :], XT[:, m, :]).then_inc(out_done, 16)
            sp.wait_ge(out_done, 16 * (4 + KD))
            sp.wait_ge(k_saved, 16)
            sp.wait_ge(ki_saved, 16)
            sp.wait_ge(v_saved, 32)

        @block.tensor
        def _(pe):
            def proj(b, k, xh, xl, mid=None, extra=None, kn=KD):
                pe.wait_ge(w_lo[b], k + 1)
                if not (isinstance(k, int) and k == 0):
                    pe.wait_ge(ps_free[b], k)
                if extra:
                    extra()
                for c in range(NCH):
                    for kk in range(kn):
                        for p, (w, x) in enumerate(((WHI, xh), (WHI, xl), (WLO, xh))):
                            last = nc.tensor.matmul(PS[b][:, c, 0:CH], w[b][:, kk, :], x[:, kk, c * CH:(c + 1) * CH],
                                                    start=(kk == 0 and p == 0), stop=(kk == kn - 1 and p == 2))
                    if c == 0 and mid:
                        mid()
                last.then_inc(mm[b], 1)

            def norm_sums(acc, r, dst):
                pe.wait_ge(n_acc, (KD - 1) * (r + 1))
                for t in range(NB):
                    w = min(P, TP - t * P)
                    last = nc.tensor.matmul(PX[0][0:w, t:t + 1], acc[:, t * P:t * P + w], CK[:, C_ONES:C_ONES + 1],
                                            start=True, stop=True)
                last.then_inc(n_sum, 1)
                pe.wait_ge(n_rc, 2 * (r + 1))
                for t in range(NB):
                    w = min(P, TP - t * P)
                    last = nc.tensor.matmul(dst[:, t // 4, (t % 4) * P:(t % 4) * P + w],
                                            RT[0:w, t:t + 1].to_broadcast([w, P]), CK[0:w, C_ID:C_ID + w], start=True, stop=True)
                last.then_inc(n_bc, 1)

            def first_proj(b, k, r):
                pe.wait_ge(w_lo[b], k + 1)
                for kk in range(KD):
                    pe.wait_ge((n_lop, n_lo)[kk % 2], 4 * r + kk // 2 + 1)
                    for c in range(NCH):
                        for p, (w, x) in enumerate(((WHI, XH), (WHI, XL), (WLO, XH))):
                            last = nc.tensor.matmul(PS[b][:, c, 0:CH], w[b][:, kk, :], x[:, kk, c * CH:(c + 1) * CH],
                                                    start=(kk == 0 and p == 0), stop=(kk == KD - 1 and p == 2))
                last.then_inc(mm[b], 1)

            pe.wait_ge(const_in, 16)
            norm_sums(ACC, 0, PS[1])
            first_proj(0, 0, 0)
            proj(1, 0, XH, XL, extra=lambda: pe.wait_ge(n_t, 8))

            def head_weights():
                pe.wait_ge(ps_free[0], 1)
                for t in range(NB):
                    w = min(P, TP - t * P)
                    last = nc.tensor.transpose(PX[t // 8][0:w, (t % 8) * 64:(t % 8) * 64 + 4],
                                               EV[0][64:68, t * P:t * P + w], CK[64:68, C_ID + 64:C_ID + 68])
                last.then_inc(wi_t, 1)

            proj(0, 1, XH, XL, head_weights)
            def decode_turn_keys(s):
                if s >= 2:
                    pe.wait_ge(kip_c, s - 1)
                pe.wait_ge(kidx_in[s], 16 * PAGES)
                for q in range(4):
                    page = s * PAGES + 2 * q
                    last = nc.tensor.transpose(PX[s % 2][:, q * P:(q + 1) * P],
                                               KIDX[:, page:page + 2, :].rearrange("p a d -> p (a d)"), ident)
                last.then_inc(kip_t, 1)

            def decode_scores(s):
                pe.wait_ge(kip_c, s + 1)
                for par in range(2):
                    last = nc.tensor.matmul(PS[par][0:32, 2, :], QZ[par * HD:(par + 1) * HD, s, :],
                                            KIP[s % 2][par * HD:(par + 1) * HD, :, :].rearrange("p q t -> p (q t)"),
                                            start=(s == 0), stop=(s == NS - 1))
                last.then_inc(di_mm, 1)

            pe.wait_ge(i_lo, 6)
            pe.wait_ge(qs_pad, 4)
            u = 0
            for b in range(2, NB):
                for h in range(IH):
                    if u < 2:
                        pe.wait_ge(ps_free[u], 2 - u)
                    else:
                        pe.wait_ge(sc_relu, u - 1)
                    if u == 3 * NS:
                        pe.wait_ge(di_relu, 1)
                    for c0 in range(0, S_W[b], 512):
                        w = min(512, S_W[b] - c0)
                        for p, keys in enumerate((KH2, KL2)):
                            last = nc.tensor.matmul(PS[u % 2][:, c0 // 512, 0:w], QS[h][:, b * P:(b + 1) * P],
                                                    keys[:, c0:c0 + w], start=(p == 0), stop=(p == 1))
                    last.then_inc(sc_mm, 1)
                    s, ride = u // 3, u % 3 == 2
                    if ride and s < NS:
                        if s == 0:
                            pe.wait_ge(wi_c, 2)
                        if s == 1:
                            pe.wait_ge(qz_c, 8)
                        decode_turn_keys(s)
                        if s >= 1:
                            decode_scores(s - 1)
                        if s == NS - 1:
                            decode_scores(s)
                    u += 1
            pe.wait_ge(sc_relu, u)
            pe.wait_ge(zz_c, 1)
            nc.tensor.transpose(PX[0][0:32, 0:LR], ZZ[:, :], CK[0:LR, C_ID:C_ID + LR]).then_inc(zz_t, 1)
            pe.wait_ge(wds_c, 1)
            pe.wait_ge(di_relu, 1)
            for c in range(2):
                last = nc.tensor.matmul(PS[1][0:LR, c, :], WDS[:, :], RD[:, c * 512:(c + 1) * 512], start=True, stop=True)
            last.then_inc(ds_mm, 1)
            ms_rows = [PX[0][0:16, 0:CH], PX[1][0:16, 0:CH], PX[0][32:48, 0:CH]]

            def head_sums(j, b, ready):
                def go():
                    pe.wait_ge(ps_free[b], ready)
                    for c in range(NCH):
                        last = nc.tensor.matmul(ms_rows[c], SELC[b][:, :], SQ[:, c * CH:(c + 1) * CH],
                                                start=isinstance(j, int) and j == 0, stop=True, skip_group_check=True)
                    last.then_inc(r_ms, 1)
                return go

            proj(1, 1, XH, XL, extra=lambda: pe.wait_ge(s8_c, 1))
            proj(0, 2, XH, XL, head_sums(0, 1, 2))
            with pe.Fori(1, 4) as i:
                proj(1, 1 + i, XH, XL, head_sums(2 * i - 1, 0, i + 2))
                proj(0, 2 + i, XH, XL, head_sums(2 * i, 1, i + 2))
            def v_turn(b, v, first):
                pe.wait_ge(ps_free[b], 6 + (v + 1) // 2)
                for q, (t0, nt) in enumerate(((0, 4), (4, 4), (8, 1))):
                    if not (first and q < 2):
                        pe.wait_ge(v_c, 3 * v + q - 1)
                    for t in range(t0, t0 + nt):
                        w = min(P, TP - t * P)
                        last = nc.tensor.transpose(PX[(3 * b + q + 1) % 2][0:w, (t - t0) * P:(t - t0 + 1) * P],
                                                   EV[b][:, t * P:t * P + w], ident)
                    last.then_inc(v_t, 1)

            proj(1, 5, XH, XL, head_sums(7, 0, 6))
            proj(0, 6, XH, XL)
            pe.wait_ge(r_rt, 3)
            v_turn(1, 0, True)
            v_turn(0, 1, False)
            proj(1, 6, XH, XL)
            proj(0, 7, XH, XL)
            v_turn(1, 2, False)
            v_turn(0, 3, False)
            pe.wait_ge(r_rc, 1)
            for j in range(8):
                b = (j + 1) % 2
                if j < 2:
                    pe.wait_ge(ps_free[b], 7 if b else 8)
                else:
                    pe.wait_ge(r_ev2, j - 1)
                for c in range(NCH):
                    last = nc.tensor.matmul(PS[b][:, c, 0:CH], SELT[:, j, :], RS[:, c * CH:(c + 1) * CH],
                                            start=True, stop=True)
                last.then_inc(r_bc, 1)
            pe.wait_ge(r_ev2, 8)
            with pe.Fori(0, 6) as i:
                proj(1, 7 + i, XH, XL)
                proj(0, 8 + i, XH, XL)
            pe.wait_ge(v_c, 12)
            pe.wait_ge(r_nrm, 8)
            for j in range(4):
                last = nc.tensor.transpose(PX[0][0:32, j * P:(j + 1) * P], QKT[:, 4 + j, 8 * P:8 * P + 32], ident)
            last.then_inc(q_t, 1)
            with pe.Fori(0, 8) as i:
                proj(1, 13 + i, XH, XL)
                proj(0, 14 + i, XH, XL)
            pe.wait_ge(ps_free[1], 21)
            pe.wait_ge(ps_free[0], 22)
            pe.wait_ge(q_c, 1)

            def qk(u, i):
                u, i = unit(u, i)
                b, e = UNITS[u]
                if u % NB == 0:
                    pe.wait_ge(hd_lo, 6 * i + 3 * e + 3)
                pe.wait_ge(a_max, NU * i + u - 1 + FREE)
                if S_W[b] > 1024:
                    pe.wait_ge(a_o, NU * i + u - 3 + FREE)
                pe.sem_inc(held, 1)
                for c0 in range(0, S_W[b], 512):
                    w = min(512, S_W[b] - c0)
                    for p, keys in enumerate((HKH, HKL)):
                        last = nc.tensor.matmul(PS[u % 2][:, c0 // 512, 0:w], HQ[e][:, b * P:(b + 1) * P],
                                                keys[e][:, c0:c0 + w], start=(p == 0), stop=(p == 1))
                last.then_inc(a_qk, 1)

            def turn(u, i):
                u, i = unit(u, i)
                b, e = UNITS[u]
                pe.wait_ge(a_exp, NU * i + u + 1)
                for t, k0, nk in BATCHES[u]:
                    pe.wait_ge(a_ta, NBAT * i + t - 1 + FREE)
                    pe.sem_inc(held, 1)
                    for kt in range(k0, k0 + nk):
                        w = min(P, S_W[b] - kt * P)
                        last = nc.tensor.transpose(PX[t % 2][0:w, (kt - k0) * P:(kt - k0) * P + ROWS[b]],
                                                   PB[u % 2][0:ROWS[b], kt * P:kt * P + w], CK[0:ROWS[b], C_ID:C_ID + ROWS[b]])
                    last.then_inc(a_tm, 1)

            def pv(u, i, extra=None):
                b, e = UNITS[u]
                t = BATCHES[u][-1][0]
                pe.wait_ge(a_ta, NBAT * i + t + 1 + FREE)
                pe.wait_ge(a_o, NU * i + u - 1 + FREE)
                if KT_N[b] == NB:
                    pe.wait_ge(a_vl, i + 1)
                if S_W[UNITS[(u + 2) % NU][0]] > 1024:
                    pe.wait_ge(a_max, NU * i + u + 3 + FREE)
                pe.sem_inc(held, 1)
                for kt in range(KT_N[b]):
                    w = min(P, S_W[b] - kt * P)
                    v = VLAST[:, e * HD:(e + 1) * HD] if kt == 8 else VT[0:w, kt, ds(i * P + e * HD, HD)]
                    last = nc.tensor.matmul(px_out[u % 2][0:ROWS[b], :], PTB[u % 2][0:w, kt, 0:ROWS[b]], v,
                                            start=(kt == 0), stop=(kt == KT_N[b] - 1))
                if extra:
                    last = extra(u, i) or last
                last.then_inc(a_pv, 1)

            def attend(i, last, extra=None):
                def more(u):
                    return u < NU or not last
                for u in range(NU):
                    if more(u + 1):
                        turn(u + 1, i)
                    decode = extra and u == 0 and i == 2
                    if decode:
                        decode_logits()
                    elif more(u + 3):
                        qk(u + 3, i)
                    pv(u, i, extra)
                    if decode:
                        pe.wait_ge(d_exp, 1)
                        qk(u + 3, i)
                        decode_turn()

            def decode_logits():
                pe.wait_ge(k_red, 32)
                pe.wait_ge(a_max, 2 * NU + 2 + FREE)
                pe.wait_ge(a_o, 2 * NU + FREE)
                pe.wait_ge(qa_c, 8)
                for p in range(PAGES):
                    dst = PS[1][0:64, p // 4, (p % 4) * P:(p % 4 + 1) * P]
                    nc.tensor.matmul(dst, CK[0:LR, C_E24:C_E24 + 64], S[0:LR, S_OFF[8] + p * P:S_OFF[8] + (p + 1) * P],
                                     start=True, stop=False)
                    nc.tensor.matmul(dst, LD[:, p, :, :].rearrange("p s h -> p (s h)"), ident, start=False, stop=True)
                new = PS[1][0:64, 2, 0:LR]
                nc.tensor.matmul(new, CK[0:LR, C_E24:C_E24 + 64],
                                 S[0:LR, S_OFF[8] + PAST:S_OFF[8] + PAST + 1].to_broadcast([LR, LR]), start=True, stop=False)
                nc.tensor.matmul(new, CK[0:64, C_ID:C_ID + 64], CK[0:64, C_NM:C_NM + LR], start=False, stop=False)
                for j in range(4):
                    last = nc.tensor.matmul(new, QA[:, j, :], QKT[:, j, 8 * P:8 * P + LR], start=False, stop=(j == 3))
                last.then_inc(d_l, 1)

            def decode_turn():
                n = sum(len(m) for m in BATCHES[0:2])
                pe.wait_ge(a_ta, 2 * NBAT + n + FREE)
                for g in range(2):
                    for p in range(4 * g, 4 * g + 4):
                        last = nc.tensor.transpose(PX[g][:, (p % 4) * 64:(p % 4 + 1) * 64], PD[:, p * P:(p + 1) * P],
                                                   CK[0:64, C_ID:C_ID + 64])
                    if g == 1:
                        last = nc.tensor.transpose(PX[1][0:LR, 256:320], PD[:, 8 * P:8 * P + LR], CK[0:64, C_ID:C_ID + 64])
                    last.then_inc(d_t, 1)
                pe.wait_ge(d_c, 3)

            def decode_values(u, i):
                if u < 2:
                    return None
                h, k = u % 2, (u - 2) // 2
                smp = 4 * (i - 2) + k // 2
                first = i == 2 and u < 4
                if h == 0:
                    pe.wait_ge(ring_in[smp % 2][k % 2], 64 * (4 + smp // 2 + 1))
                if first:
                    nc.tensor.matmul(px_dec[h], PTN[:, :], VT[0:LR, 8, h * 256:(h + 1) * 256], start=True, stop=False)
                for q in range(4):
                    p = 4 * (k % 2) + q
                    last = nc.tensor.matmul(px_dec[h], PZ[:, (p * NS + smp) * 64:(p * NS + smp + 1) * 64],
                                            RING[smp % 2][:, p, h * 256:(h + 1) * 256],
                                            start=(q == 0 and not first), stop=(q == 3))
                return last

            pe.sem_inc(a_pv, FREE)
            pe.sem_inc(a_tm, NBAT)
            qk(0, 0)
            qk(1, 0)
            turn(0, 0)
            qk(2, 0)
            with pe.Fori(0, 2) as i:
                attend(i, False)
            attend(2, False, decode_values)
            attend(3, True, decode_values)
            def out_part(b, q):
                for c in range(NCH):
                    for kk in range(4):
                        xh, xl = ((AH, AL), (COH, COL))[q]
                        for p, (w, x) in enumerate(((WHI, xh), (WHI, xl), (WLO, xh))):
                            last = nc.tensor.matmul(PS[q][:, c, 0:CH], w[b][:, 4 * q + kk, :], x[:, kk, c * CH:(c + 1) * CH],
                                                    start=(kk == 0 and p == 0), stop=(kk == 3 and p == 2))
                return last

            def outs(b, k, m):
                pe.wait_ge(w_lo[b], k + 1)
                for q in range(2):
                    pe.wait_ge((o_m0, o_m1)[q], m)
                    out_part(b, q).then_inc(mm[b] if q else o_ps, 1)

            pe.wait_ge(a_o, 4 * NU + FREE)
            for t in range(NB):
                if t >= 4:
                    pe.wait_ge(at_l, t - 3)
                for j in range(4):
                    last = nc.tensor.transpose(at_banks[t % 4][:, j * P:j * P + ROWS[t]], AT[0:ROWS[t], t, j * P:(j + 1) * P],
                                               CK[0:ROWS[t], C_ID:C_ID + ROWS[t]])
                last.then_inc(at_t, 1)
                if t == 3:
                    pe.wait_ge(d_o, 2)
                    for j in range(4):
                        last = nc.tensor.matmul(PS[0][:, 1, 8 * j:8 * j + 8], OD[:, j * P:(j + 1) * P], CK[0:64, C_OH:C_OH + 8],
                                                start=True, stop=True)
                    last.then_inc(d_at, 1)
                    pe.wait_ge(co_l, 3)
                    pe.wait_ge(co_lp, 1)
                    pe.wait_ge(w_lo[1], 22)
                    out_part(1, 1)
            pe.wait_ge(at_l, NB + 1)
            out_part(1, 0).then_inc(mm[1], 1)
            outs(0, 22, 1)
            with pe.Fori(1, 4) as i:
                outs(1, 21 + i, 2 * i)
                outs(0, 22 + i, 2 * i + 1)

            def plain(b, k, wait):
                pe.wait_ge(w_lo[b], k + 1)
                wait()
                for c in range(NCH):
                    for kk in range(KD):
                        for p, (w, x) in enumerate(((WHI, XH), (WHI, XL), (WLO, XH))):
                            last = nc.tensor.matmul(PS[b][:, c, 0:CH], w[b][:, kk, :], x[:, kk, c * CH:(c + 1) * CH],
                                                    start=(kk == 0 and p == 0), stop=(kk == KD - 1 and p == 2))
                last.then_inc(mm[b], 1)

            pe.wait_ge(w_lo[1], 26)
            pe.wait_ge(o_m1, 8)
            for kk in range(KD):
                pe.wait_ge(o_lo, kk + 1)
                for c in range(NCH):
                    for p, (w, x) in enumerate(((WHI, XH), (WHI, XL), (WLO, XH))):
                        last = nc.tensor.matmul(PS[1][:, c, 0:CH], w[1][:, kk, :], x[:, kk, c * CH:(c + 1) * CH],
                                                start=(kk == 0 and p == 0), stop=(kk == KD - 1 and p == 2))
            last.then_inc(mm[1], 1)
            plain(0, 26, lambda: pe.wait_ge(o_m0, 8))
            with pe.Fori(1, 4) as i:
                plain(1, 25 + i, lambda: pe.wait_ge(h_out, 2 * i - 1))
                plain(0, 26 + i, lambda: pe.wait_ge(h_out, 2 * i))
            pe.wait_ge(h_out, 8)
            norm_sums(HACC, 1, PS[0])

            def down(i, first):
                pe.wait_ge(f_lo, 2 * i + 2)
                pe.wait_ge(d_lo, i + 1)
                q = 0
                for m in range(KD):
                    for c in range(NCH):
                        if not (first and q < 2):
                            pe.wait_ge(d_px, 24 * i + q - 1)
                        for a in range(2):
                            for p, (w, x) in enumerate(((DHI, FH), (DHI, FL), (DLO, FH))):
                                last = nc.tensor.matmul(PX[q % 2][:, 0:CH], w[:, a, m * P:(m + 1) * P],
                                                        x[:, a, c * CH:(c + 1) * CH], start=(a == 0 and p == 0),
                                                        stop=(a == 1 and p == 2))
                        last.then_inc(d_mm, 1)
                        q += 1

            K0 = N_UP // 2

            def mixer(i, down_of, down_first):
                for a in range(2):
                    if down_of is None and a == 0:
                        first_proj(1, K0, 1)
                        plain(0, K0 + 1, lambda: pe.wait_ge(n_t, 16))
                        continue
                    plain(1, K0 + 2 * i + a, lambda: pe.wait_ge(f_g, 2 * i + a))
                    plain(0, K0 + 1 + 2 * i + a, lambda: pe.wait_ge(f_a, 2 * i + a))
                    if a == 0 and down_of is not None:
                        down(down_of, down_first)

            mixer(0, None, False)
            mixer(1, 0, True)
            with pe.Fori(2, NF // 2) as i:
                mixer(i, i - 1, False)
            down(NF // 2 - 1, False)

        @block.scalar
        def _(act):
            steps = [0]

            def step(ins):
                steps[0] += 1
                ins.then_inc(act_step, 1)
                act.wait_ge(act_step, steps[0])

            def hi(b, k):
                act.wait_ge(w_raw[b], 16 * (k + 1))
                if not (isinstance(k, int) and k == 0):
                    act.wait_ge(mm[b], k)
                nc.scalar.copy(WHI[b][:, :, :], WRAW[b][:, :, :]).then_inc(w_hi[b], 1)

            def norm_squares(src, k, sq, acc, r):
                if k >= 3:
                    act.wait_ge(n_acc, (KD - 1) * r + k - 2)
                dst = acc if k == 0 else sq[k % 2]
                nc.scalar.activation(dst[:, :], src[:, k, :], ACT.Square).then_inc(n_sq, 1)

            def norm_rest(tmp, r):
                act.wait_ge(n_sum, r + 1)
                nc.scalar.activation(RT[:, 0:8], PX[0][:, 0:8], ACT.Sqrt, bias=eps, scale=1.0 / D).then_inc(n_rt, 1)
                nc.scalar.activation(RT[0:32, 8:9], PX[0][0:32, 8:9], ACT.Sqrt, bias=eps[0:32, :], scale=1.0 / D).then_inc(n_rt, 1)
                for k in range(KD):
                    act.wait_ge(n_t, KD * r + k + 1)
                    nc.scalar.copy(XH[:, k, :], tmp[k % 4][:, :]).then_inc(n_hi, 1)

            act.wait_ge(const_in, 16)
            for k in range(KD):
                act.wait_ge(x_in[k], 16)
                norm_squares(XT, k, EV, ACC, 0)
            hi(0, 0)
            norm_rest(ROT + EV, 0)

            def swap(dst, src, done):
                for q in range(4):
                    nc.scalar.copy(dst[32 * q:32 * q + 32, :], src[32 * (q ^ 1):32 * (q ^ 1) + 32, :]).then_inc(done, 1)

            hi(1, 0)
            act.wait_ge(mm[0], 1)
            nc.scalar.copy(v3(EV[0][:, :]), ps_all[0]).then_inc(ps_free[0], 1)
            act.wait_ge(ps_free[0], 1)
            swap(ROT[0], EV[0], i_rot)
            hi(0, 1)
            act.wait_ge(i_out, 1)
            nc.scalar.copy(KH2[0:HD, :], KIO[:, :]).then_inc(i_hi, 1)
            nc.scalar.copy(KH2[HD:P, :], KIO[:, :]).then_inc(i_hi, 1)
            act.dma_start(io["o_ki"], KIO[:, :]).then_inc(ki_saved, 16)
            step(nc.scalar.mul(QZ[:, :, :].rearrange("p s c -> p (s c)"), CK[:, 0:256], 0.0))
            qzf = QZ[:, :, :].rearrange("p s c -> p (s c)")

            def query_heads(t, b):
                act.wait_ge(i_out, t + 2)
                for e in range(2):
                    rows = slice(e * HD, (e + 1) * HD)
                    nc.scalar.copy(QS[2 * t + e][rows, 0:TP], EV[b][rows, :]).then_inc(i_hi, 1)
                for half in range(2):
                    for e in range(2):
                        h = 2 * t + e
                        nc.scalar.copy(qzf[half * HD:(half + 1) * HD, h:h + 36 * 7 + 1:36],
                                       EV[b][e * HD:(e + 1) * HD, TPR:TPR + NS]).then_inc(qz_c, 1)

            act.wait_ge(mm[1], 1)
            nc.scalar.copy(v3(EV[1][:, :]), ps_all[1]).then_inc(ps_free[1], 1)
            act.wait_ge(ps_free[1], 1)
            swap(ROT[1], EV[1], i_rot)
            act.wait_ge(wi_t, 1)
            nc.scalar.mul(WI[:, 0:8, :], PX[0][:, :].rearrange("p (t c) -> p t c", c=64)[:, :, 0:4], 1.0 / 16).then_inc(wi_c, 1)
            nc.scalar.mul(WI[0:32, 8, :], PX[1][0:32, 0:4], 1.0 / 16).then_inc(wi_c, 1)
            query_heads(0, 1)
            act.wait_ge(mm[0], 2)
            nc.scalar.copy(v3(EV[0][:, :]), ps_all[0]).then_inc(ps_free[0], 1)
            act.wait_ge(ps_free[0], 2)
            swap(ROT[0], EV[0], i_rot)
            query_heads(1, 0)
            hi(1, 1)
            act.wait_ge(i_lo, 6)
            for u in range(4 * (NB - 2)):
                b = 2 + u // 4
                act.wait_ge(sc_mm, u + 1)
                if u >= 2:
                    act.wait_ge(sc_acc, u - 1)
                src = PS[u % 2][0:ROWS[b], :, :].rearrange("p c t -> p (c t)")[:, 0:S_W[b]]
                nc.scalar.activation(EV[u % 2][0:ROWS[b], 0:S_W[b]], src, ACT.Relu).then_inc(sc_relu, 1)
                s = u // 3
                if u % 3 == 2 and s < NS:
                    act.wait_ge(kip_t, s + 1)
                    if s >= 2:
                        act.wait_ge(di_mm, s - 1)
                    nc.scalar.copy(KIP[s % 2][:, :, :].rearrange("p q t -> p (q t)"), PX[s % 2][:, :]).then_inc(kip_c, 1)
                if u == 3 * NS - 1:
                    act.wait_ge(di_mm, NS)
                    for par in range(2):
                        ins = nc.scalar.activation(RD[:, :].rearrange("p (q r t) -> p r q t", r=2, t=P)[:, par, :, :],
                                                   PS[par][0:32, 2, :].rearrange("p (q t) -> p q t", t=P), ACT.Relu)
                    ins.then_inc(di_relu, 1)
            act.wait_ge(zz_t, 1)
            nc.scalar.copy(WDS[:, :], PX[0][0:32, 0:LR]).then_inc(wds_c, 1)

            def v_evac(b, k, v, wait):
                act.wait_ge(mm[b], k + 1)
                if wait:
                    act.wait_ge(v_t, 3 * (v - 1))
                nc.scalar.copy(v3(EV[b][:, :]), ps_all[b]).then_inc(ps_free[b], 1)

            def v_copy(b, v):
                for q, (t0, nt) in enumerate(((0, 4), (4, 4), (8, 1))):
                    act.wait_ge(v_t, 3 * v + q + 1)
                    px = PX[(3 * b + q + 1) % 2]
                    if q < 2:
                        src = px[:, :].rearrange("p (t d) -> p t d", t=4)
                        nc.scalar.copy(VT[:, t0:t0 + 4, v * P:(v + 1) * P], src).then_inc(v_c, 1)
                    else:
                        nc.scalar.copy(VT[0:32, 8, v * P:(v + 1) * P], px[0:32, 0:P]).then_inc(v_c, 1)

            def rope(b, k, j, first):
                act.wait_ge(mm[b], k + 1)
                if not first:
                    act.wait_ge(r_out, j - 1)
                nc.scalar.activation(v3(EV[b][:, :]), ps_all[b], ACT.Copy, scale=WV[:, ds(W_QK + j, 1)]).then_inc(r_ev, 1)
                if not (isinstance(j, int) and j == 0):
                    act.wait_ge(r_ms, j)
                nc.scalar.copy(SELC[b][:, :], CK[:, ds(C_SEL + 16 * j, 16)])
                nc.scalar.activation(v3(SQ[:, :]), ps_all[b], ACT.Square).then_inc(ps_free[b], 1)
                act.wait_ge(r_ev, j + 1)
                swap(ROT2[b], EV[b], r_rot)

            act.wait_ge(sc_acc, 4 * (NB - 2))
            act.wait_ge(ds_mm, 1)
            act.wait_ge(wv_in, 16)
            hi(0, 2)
            rope(1, 1, 0, True)
            hi(1, 2)
            rope(0, 2, 1, True)
            with act.Fori(1, 4) as i:
                hi(0, 2 + i)
                rope(1, 1 + i, 2 * i, False)
                hi(1, 2 + i)
                rope(0, 2 + i, 2 * i + 1, False)
            hi(0, 6)
            act.wait_ge(r_ms, 8)
            for c, src in enumerate((PX[0][0:16, 0:CH], PX[1][0:16, 0:CH], PX[0][32:48, 0:CH])):
                nc.scalar.activation(RS[:, c * CH:(c + 1) * CH], src, ACT.Sqrt, bias=eps[0:16, :],
                                     scale=1.0 / HD).then_inc(r_rt, 1)
            act.wait_ge(r_out, 8)
            v_evac(1, 5, 0, False)
            hi(1, 6)
            v_evac(0, 6, 1, False)
            v_copy(1, 0)
            v_copy(0, 1)
            hi(0, 7)
            v_evac(1, 6, 2, True)
            hi(1, 7)
            v_evac(0, 7, 3, True)
            v_copy(1, 2)
            v_copy(0, 3)
            act.wait_ge(v_c, 12)
            act.dma_start(io["o_v"][0:8, :, :].rearrange("t p d -> p t d"), VT[:, 0:8, :]).then_inc(v_saved, 16)
            act.dma_start(io["o_v"][8, 0:32, :], VT[0:32, 8, :]).then_inc(v_saved, 16)

            act.wait_ge(v_t, 12)
            for j in range(8):
                act.wait_ge(r_bc, j + 1)
                if j >= 2:
                    act.wait_ge(r_nrm, j - 1)
                nc.scalar.copy(v3(EV[(j + 1) % 2][:, :]), ps_all[(j + 1) % 2]).then_inc(r_ev2, 1)
            act.wait_ge(r_nrm, 8)
            act.wait_ge(ki_saved, 16)

            def conv(i, first):
                for a in range(2):
                    for q in range(3):
                        t = 3 * a + q
                        b = (1 + t) % 2
                        k = 7 + 3 * i + (t + 1) // 2
                        hi(1 - b, k if b == 0 else k + 1)
                        act.wait_ge(mm[b], k + 1)
                        j = 2 * i + a
                        if not (first and a == 0):
                            if q < 2:
                                act.wait_ge(c_u, j)
                            else:
                                act.wait_ge(c_out, j)
                        dst = (EV[0], EV[1], CB)[q]
                        nc.scalar.copy(v3(dst[:, :]), ps_all[b]).then_inc(ps_free[b], 1)
                    act.wait_ge(c_u, j + 1)
                    if not (first and a == 0):
                        act.wait_ge(c_dma, 16 * j)
                    for w in range(3):
                        nc.scalar.activation(TC[w][:, :], U[:, w:w + TP], ACT.Copy,
                                             scale=WV[:, ds(W_CW + 3 * j + w, 1)]).then_inc(c_t, 1)
                    act.wait_ge(c_t, 4 * j + 3)
                    for w in range(2):
                        nc.scalar.activation(TC[w][:, TPR:T], WV[:, ds(W_CS + 16 * j + 8 * w, 8)], ACT.Copy,
                                             scale=WV[:, ds(W_CW + 3 * j + w, 1)])
                    nc.scalar.copy(UT[:, ds(j, 1), :].rearrange("p a t -> p (a t)"), U[:, TPR:TPR + 10]).then_inc(c_t, 1)

            for i in range(2):
                conv(i, i == 0)
            act.wait_ge(c_t, 16)
            act.dma_start(io["o_u"], UT[:, :, :]).then_inc(out_done, 16)

            act.wait_ge(c_u, 4)

            def gate(b, k, i, first, hk):
                if hk is not None:
                    hi(1 - b, hk)
                act.wait_ge(mm[b], k + 1)
                if not first:
                    act.wait_ge(g_dma[b], 16 * i)
                nc.scalar.activation(v3(EV[b][:, :]), ps_all[b], ACT.Sigmoid).then_inc(ps_free[b], 1)
                act.wait_ge(ps_free[b], k + 1)
                act.dma_start(gates_d[ds(2 * i + (1 - b), 1), :, :].rearrange("a p t -> p (a t)"), EV[b][:, :]).then_inc(g_dma[b], 16)

            def head_parts(i, e):
                act.wait_ge(a_qk, NU * i + 1 if e else NU * i - NB)
                act.sem_inc(held, 1)
                parts(i, e)

            def parts(i, e):
                rows = slice(e * HD, (e + 1) * HD)
                nc.scalar.copy(HQ[e][rows, 0:TP], QKT[rows, ds(4 + i, 1), :].rearrange("p a t -> p (a t)")).then_inc(hd_hi, 1)
                for half in range(2):
                    nc.scalar.copy(HKH[e][half * HD:(half + 1) * HD, :],
                                   QKT[rows, ds(i, 1), :].rearrange("p a t -> p (a t)")).then_inc(hd_hi, 1)

            gate(1, 13, 0, True, 14)
            gate(0, 14, 0, True, 14)
            act.wait_ge(c_dma, 64)
            act.wait_ge(q_t, 1)
            nc.scalar.copy(QTOK[:, :], PX[0][0:32, :]).then_inc(q_c, 1)
            act.wait_ge(q_c, 1)
            act.dma_start(q_d.rearrange("a (s d) -> (a s) d", s=NS), QTOK[NMETA:NMETA + NS, :]).then_inc(q_dma, 16)
            nc.scalar.mul(HQ[0][:, TP:NB * P], CK[:, 0:NB * P - TP], 0.0)
            parts(0, 0)
            with act.Fori(1, 7) as i:
                gate(1, 13 + i, i, False, 14 + i)
                gate(0, 14 + i, i, False, 14 + i)
            gate(1, 20, 7, False, 21)
            gate(0, 21, 7, False, None)

            act.wait_ge(g_dma[0], 128)
            act.wait_ge(g_dma[1], 128)
            act.wait_ge(mm[1], 21)
            nc.scalar.mul(HQ[1][:, TP:NB * P], CK[:, 0:NB * P - TP], 0.0)
            step(nc.scalar.mul(QA[:, :, :].rearrange("p j c -> p (j c)"), CK[:, 0:256], 0.0))
            for j in range(4):
                for e in range(2):
                    nc.scalar.copy(QA[e * HD:(e + 1) * HD, j, 2 * j + e:2 * j + e + 57:8],
                                   QKT[e * HD:(e + 1) * HD, 4 + j, TPR:T]).then_inc(qa_c, 1)

            def t_evac(u, i):
                u, i = unit(u, i)
                b, e = UNITS[u]
                for t, k0, nk in BATCHES[u]:
                    act.wait_ge(a_tm, NBAT * (i + 1) + t + 1)
                    act.wait_ge(a_pv, NU * i + u - 1 + FREE)
                    _t_copy(nc.scalar.copy, PTB[u % 2], PX[t % 2], k0, nk, S_W[b], ROWS[b], a_ta)

            def expo(u, i):
                u, i = unit(u, i)
                b, e = UNITS[u]
                act.wait_ge(a_nm, NU * i + u + 1)
                nc.scalar.activation(PB[u % 2][0:ROWS[b], 0:S_W[b]], PB[u % 2][0:ROWS[b], 0:S_W[b]], ACT.Exp,
                                     bias=SM[0:ROWS[b], 18 + u:19 + u], scale=HD ** -0.5,
                                     accum_out=SM[0:ROWS[b], 36 + u:37 + u]).then_inc(a_exp, 1)

            def decode_expo():
                act.wait_ge(d_p, 1)
                nc.scalar.activation(PD[:, 0:PAST + LR], PS[1][0:64, :, :].rearrange("p c t -> p (c t)")[:, 0:PAST + LR], ACT.Exp,
                                     bias=SM[0:64, 56:57], scale=HD ** -0.5, accum_out=SM[0:64, 57:58]).then_inc(d_exp, 1)

            def decode_evac():
                act.wait_ge(pool_ready, 2)
                for g in range(2):
                    act.wait_ge(d_t, g + 1)
                    for p in range(4 * g, 4 * g + 4):
                        diagonal = PZ[:, p * 512:p * 512 + 576].rearrange("p (s c) -> p s c", c=72)[:, :, 0:8]
                        ins = nc.scalar.copy(diagonal, PX[g][:, (p % 4) * 64:(p % 4 + 1) * 64].rearrange("p (s h) -> p s h", h=8))
                    ins.then_inc(d_c, 1)
                nc.scalar.copy(PTN[:, :], PX[1][0:LR, 256:320]).then_inc(d_c, 1)

            def attend(i, last):
                for u in range(NU):
                    if u + 2 < NU or not last:
                        expo(u + 2, i)
                    if u + 1 < NU or not last:
                        t_evac(u + 1, i)
                    if isinstance(i, int) and i == 2 and u == 0:
                        decode_expo()
                        decode_evac()
                    if u == 1:
                        act.wait_ge(a_pv, NU * i + FREE)
                        act.sem_inc(held, 1)
                        nc.scalar.copy(VLAST[:, :], VT[0:32, 8, ds(i * P, P)]).then_inc(a_vl, 1)
                        head_parts(i, 1)
                    if u == 8 and not last:
                        head_parts(i + 1, 0)

            act.sem_inc(a_ta, FREE)
            expo(0, 0)
            expo(1, 0)
            t_evac(0, 0)
            with act.Fori(0, 2) as i:
                attend(i, False)
            attend(2, False)
            attend(3, True)
            hi(1, 21)
            act.wait_ge(a_o, 4 * NU + FREE)
            act.wait_ge(k_saved, 16)
            act.wait_ge(v_saved, 32)
            for j in range(4):
                act.wait_ge(co_in[j], 16)
                nc.scalar.copy(COH[:, j, :], CRAW[j][:, :]).then_inc(co_h, 1)
            for t in range(NB):
                act.wait_ge(at_t, t + 1)
                w = P if t < 8 else NMETA
                nc.scalar.copy(AH[:, :, t * P:t * P + w],
                               at_banks[t % 4][:, :].rearrange("p (j t) -> p j t", j=4)[:, :, 0:w]).then_inc(at_h, 1)
            act.wait_ge(d_at, 1)
            nc.scalar.copy(AH[:, :, TPR:T], PS[0][:, 1, 0:32].rearrange("p (j t) -> p j t", j=4)).then_inc(at_h, 1)
            nc.scalar.mul(AH[:, :, T:TP], CK[:, 0:32].rearrange("p (j t) -> p j t", j=4), 0.0).then_inc(at_h, 1)

            for m in range(8):
                hi(m % 2, 22 + m // 2)
                act.wait_ge(o_mix, m + 1)
                nc.scalar.copy(XH[:, m, :], MT[m % 2][:, :]).then_inc(o_hi, 1)
            for m in range(8):
                hi(m % 2, 26 + m // 2)
                act.wait_ge(h_out, m + 1)
                norm_squares(XT, m, HSQ, HACC, 1)
            norm_rest(HT_, 1)

            for b in range(2):
                step(nc.scalar.mul(G[b][:, 0:2], CK[:, 0:2], 0.0))
            K0 = N_UP // 2

            def gate_half(i, a, first):
                f = 2 * i + a
                act.wait_ge(mm[1], K0 + 1 + f)
                if not first:
                    act.wait_ge(f_cv, f - 1)
                    act.wait_ge(f_lo, f - 1)
                nc.scalar.copy(v3(G[a][:, 2:TP + 2]), ps_all[1]).then_inc(f_g, 1)
                act.wait_ge(f_g, f + 1)
                nc.scalar.copy(GT[:, ds(f, 1), :].rearrange("p a t -> p (a t)"), G[a][:, TPR:TPR + 10])
                nc.scalar.activation(TG[a][:, :], G[a][:, 0:TP], ACT.Copy,
                                     scale=WV[:, ds(W_FW + 3 * f, 1)]).then_inc(f_t0, 1)

            def silu(i, a):
                f = 2 * i + a
                act.wait_ge(f_cv, f + 1)
                nc.scalar.activation(TG[a][:, :], TG[a][:, :], ACT.Silu, bias=WV[:, ds(W_FB + f, 1)]).then_inc(f_si, 1)

            def fhi(i, a):
                f = 2 * i + a
                act.wait_ge(f_a, f + 1)
                nc.scalar.copy(FH[:, a, :], TG[a][:, :]).then_inc(f_hi, 1)

            def mixer(i, first, last):
                f = 2 * i
                hi(0, K0 + 1 + f)
                gate_half(i, 0, first)
                hi(1, K0 + 1 + f)
                silu(i, 0)
                hi(0, K0 + 2 + f)
                if not first:
                    act.wait_ge(d_mm, 24 * i)
                fhi(i, 0)
                act.wait_ge(d_raw, 16 * (i + 1))
                nc.scalar.copy(DHI[:, :, :], DRAW[:, :, :]).then_inc(d_hi, 1)
                gate_half(i, 1, first)
                if not last:
                    hi(1, K0 + 2 + f)
                silu(i, 1)
                fhi(i, 1)

            mixer(0, True, False)
            with act.Fori(1, NF // 2 - 1) as i:
                mixer(i, False, False)
            mixer(NF // 2 - 1, False, True)

        @block.gpsimd
        def _(pool):
            def lo(b, k):
                pool.wait_ge(w_hi[b], k + 1)
                nc.gpsimd.tensor_tensor(WLO[b][:, :, :], WRAW[b][:, :, :], WHI[b][:, :, :].bitcast(F32),
                                        ALU.subtract).then_inc(w_lo[b], 1)

            lo(0, 0)

            def norm_lows(tmp, r):
                for k in range(0, KD, 2):
                    pool.wait_ge(n_hi, KD * r + k + 1)
                    nc.gpsimd.tensor_tensor(XL[:, k, :], tmp[k % 4][:, :], XH[:, k, :].bitcast(F32), ALU.subtract).then_inc(n_lop, 1)

            norm_lows(ROT + EV, 0)
            pool.wait_ge(n_t, KD)
            for h in range(IH):
                nc.gpsimd.memset(QPAD[h], 0.0).then_inc(qs_pad, 1)
            pool.wait_ge(rope_in, 32)
            for t in range(3):
                if t < 2:
                    lo((t + 1) % 2, (t + 1) // 2)
                pool.wait_ge(i_rot, 4 * t + 4)
                nc.gpsimd.tensor_tensor(ROT[t % 2][:, :], ROT[t % 2][:, :], SIN[:, :], ALU.mult).then_inc(i_sin, 1)
            lo(1, 1)
            pool.wait_ge(rope2_in, 48)
            pool.wait_ge(wds_c, 1)
            pool.wait_ge(kip_c, 8)

            def rope(b, j, k):
                pool.wait_ge(r_rot, 4 * j + 4)
                nc.gpsimd.tensor_tensor(ROT2[b][:, :], ROT2[b][:, :], SIN2[:, :], ALU.mult)
                lo(b, k)
                nc.gpsimd.tensor_tensor(EV[b][:, :], EV[b][:, :], COS2[:, :], ALU.mult).then_inc(r_cos, 1)
                pool.wait_ge(r_cos, j + 1)
                nc.gpsimd.tensor_tensor(QKT[:, ds(j, 1), :].rearrange("p a t -> p (a t)"), EV[b][:, :], ROT2[b][:, :],
                                        ALU.add).then_inc(r_out, 1)

            lo(0, 2)
            with pool.Fori(0, 4) as i:
                rope(1, 2 * i, 2 + i)
                rope(0, 2 * i + 1, 3 + i)
            lo(1, 6)
            lo(0, 7)
            lo(1, 7)
            for j in range(8):
                pool.wait_ge(r_ev2, j + 1)
                nc.gpsimd.tensor_tensor(QKT[:, j, :], QKT[:, j, :], EV[(j + 1) % 2][:, :], ALU.mult).then_inc(r_nrm, 1)
            pool.wait_ge(r_nrm, 8)
            pool.dma_start(io["o_k"], QKT[:, 0:4, :]).then_inc(k_saved, 16)
            pool.wait_ge(ds_mm, 1)
            pool.wait_ge(ki_saved, 16)
            nc.gpsimd.memset(U[:, 0:2], 0.0).then_inc(pool_step, 1)

            for i in range(2):
                for a in range(2):
                    j = 2 * i + a
                    for q in range(3):
                        t = 3 * a + q
                        b = (1 + t) % 2
                        k = 7 + 3 * i + (t + 1) // 2
                        if q or j == 0:
                            lo(1 - b, k if b == 0 else k + 1)
                        if q == 1:
                            pool.wait_ge(ps_free[b], k + 1)
                            if j >= 1:
                                pool.wait_ge(c_t, 4 * j)
                            nc.gpsimd.tensor_tensor(U[:, 2:TP + 2], EV[0][:, :], EV[1][:, :], ALU.mult).then_inc(c_u, 1)
                    pool.wait_ge(c_t, 4 * j + 4)
                    st = 1 + 2 * j
                    nc.gpsimd.tensor_tensor(TC[0][:, :], TC[0][:, :], TC[1][:, :], ALU.add).then_inc(pool_step, 1)
                    lo(b, k + 1)
                    pool.wait_ge(pool_step, st + 1)
                    nc.gpsimd.tensor_tensor(TC[0][:, :], TC[0][:, :], TC[2][:, :], ALU.add).then_inc(pool_step, 1)
                    pool.wait_ge(pool_step, st + 2)
                    pool.wait_ge(ps_free[b], k + 1)
                    nc.gpsimd.tensor_tensor(TC[0][:, :], TC[0][:, :], CB[:, :], ALU.mult).then_inc(c_out, 1)
                    pool.wait_ge(c_out, j + 1)
                    pool.dma_start(conv_d[j, :, :], TC[0][:, :]).then_inc(c_dma, 16)
            lo(1, 14)

            def head_lows(i, e):
                rows, other = slice(e * HD, (e + 1) * HD), slice((1 - e) * HD, (2 - e) * HD)
                pool.wait_ge(hd_hi, 6 * i + 3 * e + 3)
                pool.sem_inc(held, 1)
                nc.gpsimd.tensor_tensor(HQ[e][other, 0:TP], QKT[rows, ds(4 + i, 1), :].rearrange("p a t -> p (a t)"),
                                        HQ[e][rows, 0:TP].bitcast(F32), ALU.subtract).then_inc(hd_lo, 1)
                for half in range(2):
                    pool.wait_ge(hd_lo, 6 * i + 3 * e + 1 + half)
                    pool.sem_inc(held, 1)
                    nc.gpsimd.tensor_tensor(HKL[e][half * HD:(half + 1) * HD, :],
                                            QKT[rows, ds(i, 1), :].rearrange("p a t -> p (a t)"),
                                            HKH[e][rows, :].bitcast(F32), ALU.subtract).then_inc(hd_lo, 1)
                pool.wait_ge(hd_lo, 6 * i + 3 * e + 3)
                pool.sem_inc(held, 1)

            with pool.Fori(1, 7) as i:
                lo(0, 14 + i)
                lo(1, 14 + i)
            lo(0, 21)
            pool.wait_ge(w_lo[0], 22)
            head_lows(0, 0)

            def sample(s, b):
                for p in range(PAGES):
                    if p % 4 == 0:
                        pool.wait_ge(ring_in[b][p // 4], 64 * s + 64)
                        pool.sem_inc(held, 1)
                    nc.gpsimd.tensor_tensor(RING[b][:, p, :], RING[b][:, p, :],
                                            QB[:, ds(2 * s + b, 1), :].rearrange("p a d -> p (a d)"),
                                            ALU.mult).then_inc(k_prod, 1)

            pool.wait_ge(qb_in, 16)
            with pool.Fori(0, 2) as i:
                sample(2 * i, 0)
                sample(2 * i, 1)
                pool.wait_ge(k_prod, 32 * i + 16)
                head_lows(i, 1)
                pool.wait_ge(qb_rest, 16)
                sample(2 * i + 1, 0)
                sample(2 * i + 1, 1)
                pool.wait_ge(k_prod, 32 * i + 32)
                head_lows(i + 1, 0)
            for g in range(2):
                nc.gpsimd.memset(PZ[:, 2080 * g:2080 * (g + 1)], 0.0).then_inc(pool_ready, 1)
            pool.wait_ge(pool_ready, 2)
            head_lows(2, 1)
            head_lows(3, 0)
            head_lows(3, 1)
            lo(1, 21)
            pool.wait_ge(co_h, 3)
            nc.gpsimd.tensor_tensor(COL[:, 2, :], CRAW[2][:, :], COH[:, 2, :].bitcast(F32), ALU.subtract).then_inc(co_lp, 1)
            pool.wait_ge(d_at, 1)
            lo(0, 22)
            for n in range(N_O + 2, N_UP + 1):
                lo(n % 2, n // 2)
            norm_lows(HT_, 1)
            K0 = N_UP // 2

            def dlo(i):
                pool.wait_ge(d_hi, i + 1)
                nc.gpsimd.tensor_tensor(DLO[:, :, :], DRAW[:, :, :], DHI[:, :, :].bitcast(F32), ALU.subtract).then_inc(d_lo, 1)

            def mixer(i, last):
                lo(0, K0 + 1 + 2 * i)
                lo(1, K0 + 1 + 2 * i)
                lo(0, K0 + 2 + 2 * i)
                dlo(i)
                if not last:
                    lo(1, K0 + 2 + 2 * i)

            with pool.Fori(0, NF // 2 - 1) as i:
                mixer(i, False)
            mixer(NF // 2 - 1, True)

        @block.vector
        def _(dve):
            steps = [0]

            def step(ins):
                steps[0] += 1
                ins.then_inc(dve_step, 1)
                dve.wait_ge(dve_step, steps[0])

            def norm_add(k, sq, acc, r):
                if k == 0:
                    return
                dve.wait_ge(n_sq, KD * r + k + 1)
                if k >= 2:
                    dve.wait_ge(n_acc, (KD - 1) * r + k - 1)
                nc.vector.tensor_tensor(acc[:, :], acc[:, :], sq[k % 2][:, :], ALU.add).then_inc(n_acc, 1)

            def norm_rest(src, tmp, wcol, r, ps):
                dve.wait_ge(n_rt, 2 * (r + 1))
                nc.vector.reciprocal(RT[:, 0:8], RT[:, 0:8]).then_inc(n_rc, 1)
                nc.vector.reciprocal(RT[0:32, 8:9], RT[0:32, 8:9]).then_inc(n_rc, 1)
                dve.wait_ge(n_bc, r + 1)
                rms = ps[:, :, :].rearrange("p c t -> p (c t)")[:, 0:TP]

                def low(k):
                    dve.wait_ge(n_hi, KD * r + k + 1)
                    nc.vector.tensor_tensor(XL[:, k, :], tmp[k % 4][:, :], XH[:, k, :].bitcast(F32), ALU.subtract).then_inc(n_lo, 1)

                for k in range(KD):
                    if k >= 4:
                        dve.wait_ge((n_lop, n_lo)[k % 2], 4 * r + k // 2 - 1)
                    nc.vector.scalar_tensor_tensor(out=tmp[k % 4][:, :], in0=src[:, k, :], scalar=WV[:, wcol + k:wcol + k + 1],
                                                   in1=rms, op0=ALU.mult, op1=ALU.mult).then_inc(n_t, 1)
                    if k >= 2 and k % 2 == 0:
                        low(k - 1)
                low(KD - 1)

            for k in range(KD):
                norm_add(k, EV, ACC, 0)
            dve.wait_ge(wv_in, 16)
            norm_rest(XT, ROT + EV, W_AN, 0, PS[1])

            dve.wait_ge(rope_in, 32)

            def rope(b, t, out, rows):
                dve.wait_ge(i_rot, 4 * t + 4)
                nc.vector.tensor_tensor(EV[b][0:rows, :], EV[b][0:rows, :], COS[0:rows, :], ALU.mult).then_inc(i_cos, 1)
                dve.wait_ge(i_cos, t + 1)
                dve.wait_ge(i_sin, t + 1)
                nc.vector.tensor_tensor(out, EV[b][0:rows, :], ROT[b][0:rows, :], ALU.add).then_inc(i_out, 1)

            rope(0, 0, KIO[:, :], HD)
            dve.wait_ge(i_hi, 2)
            for half in range(2):
                nc.vector.tensor_tensor(KL2[half * HD:(half + 1) * HD, :], KIO[:, :], KH2[0:HD, :].bitcast(F32),
                                        ALU.subtract).then_inc(i_lo, 1)
            for t in range(2):
                b = (t + 1) % 2
                rope(b, t + 1, EV[b][:, :], P)
                for e in range(2):
                    rows, other = slice(e * HD, (e + 1) * HD), slice((1 - e) * HD, (2 - e) * HD)
                    dve.wait_ge(i_hi, 2 * t + e + 3)
                    nc.vector.tensor_tensor(QS[2 * t + e][other, 0:TP], EV[b][rows, :], QS[2 * t + e][rows, 0:TP].bitcast(F32),
                                            ALU.subtract).then_inc(i_lo, 1)
            dve.wait_ge(wi_c, 2)
            u = 0
            for b in range(2, NB):
                s = S[0:ROWS[b], S_OFF[b]:S_OFF[b] + S_W[b]]
                for h in range(IH):
                    dve.wait_ge(sc_relu, u + 1)
                    r = EV[u % 2][0:ROWS[b], 0:S_W[b]]
                    w = WI[0:ROWS[b], b, h:h + 1]
                    if h == 0:
                        ins = nc.vector.tensor_scalar(s, r, w, 0.0, ALU.mult, ALU.add)
                    else:
                        ins = nc.vector.scalar_tensor_tensor(out=s, in0=r, scalar=w, in1=s, op0=ALU.mult, op1=ALU.add)
                    ins.then_inc(sc_acc, 1)
                    dve.wait_ge(sc_acc, u + 1)
                    u += 1
                if b < 8:
                    d = S[:, S_OFF[b] + b * P:S_OFF[b] + (b + 1) * P]
                    step(nc.vector.tensor_tensor(d, d, CK[:, C_CM:C_CM + P], ALU.add))
            nc.vector.tensor_tensor(ZZ[:, :].rearrange("p (s h) -> p s h", h=4),
                                    CK[0:LR, C_ZP:C_ZP + 32].rearrange("p (s h) -> p s h", h=4),
                                    WI[0:LR, 8:9, :].to_broadcast([LR, 8, 4]), ALU.mult).then_inc(zz_c, 1)
            s8 = S_OFF[8]
            step(nc.vector.tensor_tensor(SM[0:LR, 0:8], S[0:LR, s8 + TPR:s8 + T], CK[0:LR, C_DIAG:C_DIAG + 8], ALU.mult))
            step(nc.vector.reduce_sum(SM[0:LR, 8:9], SM[0:LR, 0:8], AX.X))
            step(nc.vector.tensor_scalar(S[0:LR, s8:s8 + TP], S[0:LR, s8:s8 + TP], CK[0:LR, C_ROWP:C_ROWP + 1], None, ALU.mult))
            step(nc.vector.tensor_tensor(S[0:LR, s8 + 1024:s8 + 1025], S[0:LR, s8 + 1024:s8 + 1025], SM[0:LR, 8:9], ALU.add))
            step(nc.vector.tensor_tensor(S[0:LR, s8 + 1024:s8 + TP], S[0:LR, s8 + 1024:s8 + TP], CK[0:LR, C_CM8:C_CM8 + 32], ALU.add))
            dve.wait_ge(ds_mm, 1)
            s8v = S[0:LR, s8:s8 + 1024].rearrange("p (c t) -> p c t", t=512)
            nc.vector.tensor_tensor(s8v, s8v, PS[1][0:LR, 0:2, :], ALU.add).then_inc(s8_c, 1)
            dve.wait_ge(s8_c, 1)
            def topk(blocks):
                base = steps[0]
                n = len(blocks)
                last = {}
                for _ in range(TOPK // 8):
                    for what in range(2):
                        for x, b in enumerate(blocks):
                            s = S[0:ROWS[b], S_OFF[b]:S_OFF[b] + S_W[b]]
                            if x in last:
                                dve.wait_ge(dve_step, last[x])
                            if what == 0:
                                ins = nc.vector.max(M8[x][0:ROWS[b], :], s)
                            else:
                                ins = nc.vector.match_replace(s, M8[x][0:ROWS[b], :], s, TAKEN)
                            ins.then_inc(dve_step, 1)
                            steps[0] += 1
                            last[x] = steps[0]
                dve.wait_ge(dve_step, steps[0])

            topk([7, 2])
            dve.wait_ge(r_rt, 3)
            nc.vector.reciprocal(RS[:, :], RS[:, :]).then_inc(r_rc, 1)
            topk([6, 3])
            topk([5, 4])
            topk([8])
            for b in range(2, NB):
                s = S[0:ROWS[b], S_OFF[b]:S_OFF[b] + S_W[b]]
                nc.vector.tensor_scalar(s, s, 0.5 * TAKEN, NEG, ALU.is_gt, ALU.mult)

            def logits(u, i):
                u, i = unit(u, i)
                b, e = UNITS[u]
                r, w = ROWS[b], S_W[b]
                dve.wait_ge(a_qk, NU * i + u + 1)
                before = BATCHES[(u - 2) % NU][-1][0] + 1
                dve.wait_ge(a_tm, NBAT * (i + 1) + before if u >= 2 else NBAT * i + before)
                dve.sem_inc(held, 1)
                if b < 2:
                    if b == 1:
                        nc.vector.tensor_copy(PB[u % 2][:, 0:P], PS[u % 2][:, 0, 0:P])
                    nc.vector.tensor_tensor(PB[u % 2][:, b * P:w], PS[u % 2][:, 0, b * P:w], CK[:, C_CM:C_CM + P],
                                            ALU.add).then_inc(a_lg, 1)
                    dve.wait_ge(a_lg, 4 * i + 2 * e + b + 1)
                    nc.vector.reduce_max(SM[:, u:u + 1], PB[u % 2][:, 0:w], AX.X).then_inc(a_max, 1)
                else:
                    flat = PS[u % 2][0:r, :, :].rearrange("p c t -> p (c t)")[:, 0:w]
                    nc.vector.tensor_tensor_reduce(PB[u % 2][0:r, 0:w], flat, S[0:r, S_OFF[b]:S_OFF[b] + w], 1.0, -3.0e38,
                                                   ALU.add, ALU.max, SM[0:r, u:u + 1]).then_inc(a_max, 1)
                dve.wait_ge(a_max, NU * i + u + 1 + FREE)
                nc.vector.tensor_scalar(SM[0:r, 18 + u:19 + u], SM[0:r, u:u + 1], -(HD ** -0.5), None, ALU.mult).then_inc(a_nm, 1)

            def out(u, i):
                b, e = UNITS[u]
                r = ROWS[b]
                dve.wait_ge(a_exp, NU * i + u + 1)
                nc.vector.reciprocal(SM[0:r, 36 + u:37 + u], SM[0:r, 36 + u:37 + u]).then_inc(a_rc, 1)
                dve.wait_ge(a_rc, NU * i + u + 1)
                dve.wait_ge(a_pv, NU * i + u + 1 + FREE)
                ins = nc.vector.tensor_scalar(AT[0:r, b, ds(i * P + e * HD, HD)], px_out[u % 2][0:r, :],
                                              SM[0:r, 36 + u:37 + u], None, ALU.mult)
                if isinstance(i, int) and i >= 2 and u >= 2:
                    od = OD[:, (u % 2) * 256:(u % 2 + 1) * 256]
                    if i == 2 and u < 4:
                        ins = nc.vector.tensor_copy(od, px_dec[u % 2])
                    else:
                        dve.wait_ge(a_o, NU * i + u - 1 + FREE)
                        ins = nc.vector.tensor_tensor(od, od, px_dec[u % 2], ALU.add)
                ins.then_inc(a_o, 1)

            def reduce_pages(u, i):
                k = (u - 2) // 4
                b, p = k % 2, 2 * ((u - 2) % 4)
                dve.wait_ge(k_prod, 32 * i + 2 * u - 2)
                dve.sem_inc(held, 1)
                for q in range(2):
                    ins = nc.vector.reduce_sum(LD[:, p + q, ds(4 * i + k, 1), :].rearrange("p a h -> p (a h)"),
                                               RING[b][:, p + q, :].rearrange("p (h d) -> p h d", d=HD), AX.X)
                ins.then_inc(k_red, 1)

            def attend(i, last, keys=False):
                for u in range(NU):
                    if u + 2 < NU or not last:
                        logits(u + 2, i)
                    if u >= 1:
                        out(u - 1, i)
                    if keys and u >= 2:
                        reduce_pages(u, i)
                    if isinstance(i, int) and i == 2 and u == 0:
                        decode_max()
                out(NU - 1, i)

            def decode_max():
                dve.wait_ge(d_l, 1)
                step(nc.vector.reduce_max(SM[0:64, 54:55], PS[1][0:64, :, :].rearrange("p c t -> p (c t)")[:, 0:PAST + LR], AX.X))
                nc.vector.tensor_scalar(SM[0:64, 56:57], SM[0:64, 54:55], -(HD ** -0.5), None, ALU.mult).then_inc(d_p, 1)

            for s, n in ((a_max, FREE), (a_o, FREE)):
                dve.sem_inc(s, n)
            dve.wait_ge(g_dma[0], 128)
            dve.wait_ge(g_dma[1], 128)
            logits(0, 0)
            logits(1, 0)
            with dve.Fori(0, 2) as i:
                attend(i, False, True)
            attend(2, False)
            attend(3, True)
            dve.wait_ge(d_exp, 1)
            step(nc.vector.reciprocal(SM[0:64, 58:59], SM[0:64, 57:58]))
            dve.wait_ge(a_o, 4 * NU + FREE)
            for h in range(2):
                cols = slice(h * 256, (h + 1) * 256)
                nc.vector.scalar_tensor_tensor(out=OD[:, cols], in0=OD[:, cols], scalar=SM[0:64, 58:59],
                                               in1=CK[0:64, C_BD + h * 256:C_BD + (h + 1) * 256],
                                               op0=ALU.mult, op1=ALU.mult).then_inc(d_o, 1)
            for j in (0, 1, 3):
                dve.wait_ge(co_h, j + 1)
                nc.vector.tensor_tensor(COL[:, j, :], CRAW[j][:, :], COH[:, j, :].bitcast(F32), ALU.subtract).then_inc(co_l, 1)
            for t in range(NB):
                dve.wait_ge(at_h, t + 1)
                w = P if t < 8 else NMETA
                nc.vector.tensor_tensor(AL[:, :, t * P:t * P + w], at_banks[t % 4][:, :].rearrange("p (j t) -> p j t", j=4)[:, :, 0:w],
                                        AH[:, :, t * P:t * P + w].bitcast(F32), ALU.subtract).then_inc(at_l, 1)
            dve.wait_ge(at_h, NB + 2)
            step(nc.vector.tensor_tensor(AL[:, :, TPR:T], PS[0][:, 1, 0:32].rearrange("p (j t) -> p j t", j=4),
                                         AH[:, :, TPR:T].bitcast(F32), ALU.subtract))
            nc.vector.tensor_copy(AL[:, :, T:TP], AH[:, :, T:TP].bitcast(F32)).then_inc(at_l, 1)
            for m in range(8):
                b = m % 2
                dve.wait_ge(*((o_ps, m) if m else (mm[1], 22)))
                dve.wait_ge(sg_in[b], 32 * (m // 2 + 1))
                if m >= 2:
                    dve.wait_ge(o_lo, m - 1)
                nc.vector.tensor_tensor(v3(MT[b][:, :]), v3(SGA[b][:, :]), ps_all[0], ALU.mult).then_inc(o_m0, 1)
                dve.wait_ge(mm[1 - b], 22 + m // 2 + b)
                nc.vector.tensor_tensor(v3(SGC[b][:, :]), v3(SGC[b][:, :]), ps_all[1], ALU.mult).then_inc(o_m1, 1)
                dve.wait_ge(o_m1, m + 1)
                nc.vector.tensor_tensor(MT[b][:, :], MT[b][:, :], SGC[b][:, :], ALU.add).then_inc(o_mix, 1)
                dve.wait_ge(o_hi, m + 1)
                nc.vector.tensor_tensor(XL[:, m, :], MT[b][:, :], XH[:, m, :].bitcast(F32), ALU.subtract).then_inc(o_lo, 1)
            for m in range(8):
                b = (N_MERGE + m) % 2
                dve.wait_ge(mm[b], (N_MERGE + m) // 2 + 1)
                dve.wait_ge(xr_in[m % 2], 16 * (m // 2 + 1))
                nc.vector.tensor_tensor(v3(XT[:, m, :]), v3(XR[m % 2][:, :]), ps_all[b], ALU.add).then_inc(h_out, 1)
                norm_add(m, HSQ, HACC, 1)
            norm_rest(XT, HT_, W_FN, 1, PS[0])

            K0 = N_UP // 2

            def conv(i, a):
                f = 2 * i + a
                w = [WV[:, ds(W_FW + 3 * f + q, 1)] for q in range(3)]
                dve.wait_ge(f_t0, f + 1)
                nc.vector.scalar_tensor_tensor(out=TG[a][:, :], in0=G[a][:, 1:TP + 1], scalar=w[1], in1=TG[a][:, :],
                                               op0=ALU.mult, op1=ALU.add).then_inc(f_s, 1)
                dve.wait_ge(f_s, 4 * f + 1)
                nc.vector.scalar_tensor_tensor(out=TG[a][:, :], in0=G[a][:, 2:TP + 2], scalar=w[2], in1=TG[a][:, :],
                                               op0=ALU.mult, op1=ALU.add).then_inc(f_s, 1)
                dve.wait_ge(f_s, 4 * f + 2)
                d = TG[a][:, TPR:T]
                nc.vector.tensor_scalar(d, WV[:, ds(W_FS + 16 * f, 8)], w[0], None, ALU.mult).then_inc(f_s, 1)
                dve.wait_ge(f_s, 4 * f + 3)
                nc.vector.scalar_tensor_tensor(out=d, in0=WV[:, ds(W_FS + 16 * f + 8, 8)], scalar=w[1], in1=d,
                                               op0=ALU.mult, op1=ALU.add).then_inc(f_s, 1)
                dve.wait_ge(f_s, 4 * f + 4)
                nc.vector.scalar_tensor_tensor(out=d, in0=G[a][:, TPR + 2:T + 2], scalar=w[2], in1=d,
                                               op0=ALU.mult, op1=ALU.add).then_inc(f_cv, 1)

            def times_val(i, a):
                f = 2 * i + a
                dve.wait_ge(f_si, f + 1)
                dve.wait_ge(mm[0], K0 + 2 + f)
                nc.vector.tensor_tensor(v3(TG[a][:, :]), v3(TG[a][:, :]), ps_all[0], ALU.mult).then_inc(f_a, 1)

            def flo(i, a):
                f = 2 * i + a
                dve.wait_ge(f_hi, f + 1)
                nc.vector.tensor_tensor(FL[:, a, :], TG[a][:, :], FH[:, a, :].bitcast(F32), ALU.subtract).then_inc(f_lo, 1)

            def down(i):
                q = 0
                for m in range(KD):
                    for c in range(NCH):
                        dve.wait_ge(d_mm, 24 * i + q + 1)
                        h = XT[:, m, c * CH:(c + 1) * CH]
                        nc.vector.tensor_tensor(h, h, PX[q % 2][:, 0:CH], ALU.add).then_inc(d_px, 1)
                        q += 1

            def mixer(i, first):
                conv(i, 0)
                times_val(i, 0)
                if not first:
                    down(i - 1)
                flo(i, 0)
                conv(i, 1)
                times_val(i, 1)
                flo(i, 1)

            mixer(0, True)
            with dve.Fori(1, NF // 2) as i:
                mixer(i, False)
            down(NF // 2 - 1)


def _constants():
    pos = np.concatenate([np.arange(TPR), np.full(TP - TPR, PAST)]).astype(np.float32)
    freqs = (10000.0 ** (-np.arange(32, dtype=np.float64) / 32)).astype(np.float32)
    ang = (pos[None, :] * freqs[:, None]).astype(np.float32)
    cos, sin = np.cos(ang), np.sin(ang)
    cos = np.concatenate([cos, cos, cos, cos]).astype(np.float32)
    sin = np.concatenate([-sin, sin, -sin, sin]).astype(np.float32)
    ck = np.zeros((P, C_END), np.float32)
    ck[:, C_ID:C_ID + P] = np.eye(P)
    ck[:, C_ONES:C_ONES + P] = 1.0
    r = np.arange(P)
    ck[:, C_CM:C_CM + P] = np.where(r[None, :] <= r[:, None], 0.0, NEG)
    for s in range(NS):
        ck[16 + s, C_E24 + 8 * s:C_E24 + 8 * s + 8] = 1.0
        ck[8 * s:8 * s + 8, C_OH + s] = 1.0
        ck[16 + s, C_DIAG + s] = 1.0
        ck[16 + s, C_ZP + 4 * s:C_ZP + 4 * s + 4] = 1.0
    ck[0:64, C_NM:C_NM + LR] = NEG
    for s in range(NS):
        for h in range(NH):
            ck[8 * s + h, C_BD + HD * h:C_BD + HD * (h + 1)] = 1.0
            ck[8 * s + h, C_NM + 16 + s] = 0.0
    ck[0:16, C_ROWP] = 1.0
    ck[:, C_EPS] = EPS
    ck[0:LR, C_CM8:C_CM8 + 32] = NEG
    for q in range(16):
        ck[q, C_CM8:C_CM8 + q + 1] = 0.0
    ck[16:LR, C_CM8] = 0.0
    selt = np.zeros((16, 8, P), np.float32)
    for j in range(8):
        ck[0:64, C_SEL + 16 * j + 2 * j] = 1.0
        ck[64:128, C_SEL + 16 * j + 2 * j + 1] = 1.0
        selt[2 * j, j, 0:64] = 1.0
        selt[2 * j + 1, j, 64:128] = 1.0
    return cos, sin, ck, selt


def _column_tiles(w, starts):
    k = w.shape[0] // P
    return np.stack([w[:, c:c + P].reshape(k, P, P).transpose(1, 0, 2).reshape(P, k * P) for c in starts])


def _by_feature(v, n):
    v = v.reshape(v.shape[:-1] + (n, P))
    return np.moveaxis(np.moveaxis(v, -1, 0), -1, 1)


def kernel(x_prompt, x_sample, cache_k, cache_v, cache_kidx, state_conv, state_ffn_conv, page_table,
           meta_tokens, attn_norm_w, w_in, q_norm_w, k_norm_w, conv_w, w_o_attn, w_o_conv, w_merge,
           ffn_norm_w, w_up, ffn_conv_w, ffn_conv_b, w_down):
    import concourse.bacc as bacc
    from concourse.bass_utils import run_bass_kernel_spmd

    f = np.float32
    x = np.concatenate([np.asarray(meta_tokens), np.asarray(x_prompt)[0], np.asarray(x_sample)[:, 0],
                        np.zeros((TP - T, D), f)])
    xt = np.ascontiguousarray(x.reshape(TP, KD, P).transpose(2, 1, 0))
    w_in = np.asarray(w_in)[0]
    q0, k0, v0, i0, ki0, cx0 = 0, 512, 1024, 1536, 1792, 1860
    cb0, cc0, ga0, gc0 = cx0 + 512, cx0 + 1024, cx0 + 1536, cx0 + 2560
    cols = [ki0, i0, i0 + P] + [k0 + P * j for j in range(4)] + [q0 + P * j for j in range(4)]
    cols += [v0 + P * j for j in range(4)]
    for j in range(4):
        cols += [cx0 + P * j, cc0 + P * j, cb0 + P * j]
    cols += [ga0 + P * j for j in range(8)] + [gc0 + P * j for j in range(8)]
    eight = [P * j for j in range(8)]
    w_up = np.asarray(w_up)[0]
    wtiles = np.concatenate([
        _column_tiles(w_in, cols),
        np.concatenate([_column_tiles(np.asarray(w_o_attn)[0], eight), _column_tiles(np.asarray(w_o_conv)[0], eight)], axis=2),
        _column_tiles(np.asarray(w_merge)[0], eight),
        _column_tiles(w_up, [P * (j // 2) + DFF * (j % 2) for j in range(2 * NF)]),
    ])
    wdown = np.asarray(w_down)[0].reshape(NF, P, D)
    qk = np.stack([np.tile(np.asarray(k_norm_w)[0], 2)] * 4 + [np.tile(np.asarray(q_norm_w)[0], 2)] * 4, axis=1)
    st_c, st_f = np.asarray(state_conv)[0], np.asarray(state_ffn_conv)[0]
    smallw = np.ascontiguousarray(np.concatenate([
        _by_feature(np.asarray(attn_norm_w)[0], 8), _by_feature(np.asarray(ffn_norm_w)[0], 8), qk,
        _by_feature(np.asarray(conv_w)[0], 4).reshape(P, -1),
        _by_feature(st_c.transpose(1, 0, 2), 4).reshape(P, -1),
        _by_feature(np.asarray(ffn_conv_w)[0], NF).reshape(P, -1),
        _by_feature(np.asarray(ffn_conv_b)[0], NF),
        _by_feature(st_f.transpose(1, 0, 2), NF).reshape(P, -1)], axis=1))
    cos, sin, ck, selt = _constants()
    n_phys = cache_k.shape[1]
    arrays = {
        "xT": xt, "wtiles": wtiles, "wdown": wdown, "smallw": smallw, "consts": ck, "cos": cos, "sin": sin, "selt": selt,
        "cache_k": np.asarray(cache_k)[0].reshape(n_phys, P, 512), "cache_v": np.asarray(cache_v)[0].reshape(n_phys, P, 512),
        "cache_kidx": np.asarray(cache_kidx)[0], "page_table": np.asarray(page_table).reshape(1, NS * PAGES),
        "state_conv": st_c, "state_ffn": st_f,
    }
    outs = {"y": (P, KD, TP), "o_k": (P, 4, TP), "o_v": (NB, P, 512), "o_ki": (HD, TP), "o_u": (P, 4, 10),
            "o_g": (P, NF, 10), "o_cst": (NS, 512), "o_fst": (NS, DFF)}
    nc = bacc.Bacc("TRN2", target_bir_lowering=False, num_devices=1)
    io = {}
    for name, a in arrays.items():
        a = arrays[name] = np.ascontiguousarray(a)
        io[name] = nc.dram_tensor(name, a.shape, mybir.dt.from_np(a.dtype), kind="ExternalInput").ap()
    for name, shape in outs.items():
        io[name] = nc.dram_tensor(name, shape, F32, kind="ExternalOutput").ap()
    build(nc, io)
    r = run_bass_kernel_spmd(nc, [arrays], core_ids=[0]).results[0]
    y = r["y"].transpose(2, 1, 0).reshape(TP, D)
    kk = r["o_k"].transpose(2, 1, 0).reshape(TP, NH, HD)
    vv = r["o_v"].reshape(NB * P, NH, HD)
    ki = r["o_ki"].transpose(1, 0)
    u = r["o_u"].transpose(2, 1, 0).reshape(10, 512)
    g = r["o_g"].transpose(2, 1, 0).reshape(10, DFF)
    return (y[NMETA:TPR][None], y[TPR:T][:, None],
            kk[None, None, :TPR], vv[None, None, :TPR], ki[None, None, :TPR], u[None, None, 0:2], g[None, None, 0:2],
            kk[TPR:T][None, :, None], vv[TPR:T][None, :, None], ki[TPR:T][None, :, None],
            np.stack([r["o_cst"], u[2:]], axis=1)[None], np.stack([r["o_fst"], g[2:]], axis=1)[None])
```
